# Optimizing a Trainium2 kernel written in Bass

```python
import jax, jax.numpy as jnp
from jax import lax
import numpy as np

D_MODEL = 2048
BATCH = 1
SEQ = 128
DEPTH = 1
DEC_BATCH = 1
DEC_SEQ = 512
PAST_LEN = 256

GRID_W = 64
N_HEADS = 16
N_KV_HEADS = 4
HEAD_DIM = 128
Q_GROUP = N_HEADS // N_KV_HEADS
ATTN_WIDTH = N_HEADS * HEAD_DIM
KV_WIDTH = N_KV_HEADS * HEAD_DIM
WINDOW = 128
BLOCK = 128
CONV_WIDTH = D_MODEL // 2
CONV_KERNEL = 31
N_EXPERTS = 16
D_EXPERT = D_MODEL // 2
EC_FACTOR = 2
ROPE_BASE = 10000.0
EPS = 1e-6
N_MOD = 6
NEG = -1e30
SPLITS = (2 * CONV_WIDTH,
          2 * CONV_WIDTH + ATTN_WIDTH,
          2 * CONV_WIDTH + ATTN_WIDTH + KV_WIDTH,
          2 * CONV_WIDTH + ATTN_WIDTH + 2 * KV_WIDTH,
          2 * CONV_WIDTH + ATTN_WIDTH + 2 * KV_WIDTH + D_MODEL)
IN_COLS = 2 * CONV_WIDTH + ATTN_WIDTH + 2 * KV_WIDTH + 2 * D_MODEL

kernel_name = "hybrid_diffusion_conformer_swa_ec_step"

def rmsnorm(x, g):
    xf = x.astype(jnp.float32)
    y = xf * lax.rsqrt(jnp.mean(xf * xf, axis=-1, keepdims=True) + EPS)
    return y.astype(x.dtype) * g

def modulate_params(cond, w_ada, b_ada):
    m = jax.nn.silu(cond) @ w_ada + b_ada
    return jnp.split(m[:, None, :], N_MOD, axis=-1)

def rope_2d(x):
    n = x.shape[1]
    rows = n // GRID_W
    row = jnp.broadcast_to(jnp.arange(rows)[:, None], (rows, GRID_W)).reshape(-1).astype(jnp.float32)
    col = jnp.broadcast_to(jnp.arange(GRID_W)[None, :], (rows, GRID_W)).reshape(-1).astype(jnp.float32)
    half = HEAD_DIM // 2
    quarter = half // 2
    inv = ROPE_BASE ** (-jnp.arange(quarter, dtype=jnp.float32) / quarter)

    def rot(xh, pos):
        ang = pos[:, None] * inv[None, :]
        cos = jnp.cos(ang)[None, :, None, :]
        sin = jnp.sin(ang)[None, :, None, :]
        x1 = xh[..., :quarter].astype(jnp.float32)
        x2 = xh[..., quarter:].astype(jnp.float32)
        return jnp.concatenate([x1 * cos - x2 * sin, x1 * sin + x2 * cos], axis=-1)

    out = jnp.concatenate([rot(x[..., :half], row), rot(x[..., half:], col)], axis=-1)
    return out.astype(x.dtype)

def conformer_conv(u, w_dw, b_dw, ln_g, ln_b, w_pw2):
    a, gt = jnp.split(u, 2, axis=-1)
    z = a * jax.nn.sigmoid(gt)
    pad = CONV_KERNEL // 2
    z = lax.conv_general_dilated(z, w_dw[:, None, :], window_strides=(1,),
                                 padding=[(pad, pad)],
                                 dimension_numbers=('NWC', 'WIO', 'NWC'),
                                 feature_group_count=CONV_WIDTH) + b_dw
    zf = z.astype(jnp.float32)
    mu = jnp.mean(zf, axis=-1, keepdims=True)
    var = jnp.mean(jnp.square(zf - mu), axis=-1, keepdims=True)
    z = ((zf - mu) * lax.rsqrt(var + EPS)).astype(z.dtype) * ln_g + ln_b
    return jax.nn.silu(z) @ w_pw2

def sink_softmax_av(sc, vals, sink):
    sk = sink.astype(jnp.float32).reshape(N_KV_HEADS, Q_GROUP)[None, :, :, None, None]
    m = jnp.maximum(jnp.max(sc, axis=-1, keepdims=True), sk)
    p = jnp.exp(sc - m)
    den = jnp.sum(p, axis=-1, keepdims=True) + jnp.exp(sk - m)
    w = (p / den).astype(vals.dtype)
    return jnp.einsum('bkgqs,bskd->bqkgd', w, vals)

def context_attention(q, k, v, sink):
    b, s = q.shape[:2]
    nb = s // BLOCK
    scale = HEAD_DIM ** -0.5
    qb = q.reshape(b, nb, BLOCK, N_KV_HEADS, Q_GROUP, HEAD_DIM).transpose(1, 0, 2, 3, 4, 5)

    def one(qblk):
        sc = jnp.einsum('bqkgd,bskd->bkgqs', qblk, k).astype(jnp.float32) * scale
        return sink_softmax_av(sc, v, sink)

    out = lax.map(one, qb)
    return out.transpose(1, 0, 2, 3, 4, 5).reshape(b, s, ATTN_WIDTH)

def latent_attention(q, k, v, ck, cv, sink):
    b, n = q.shape[:2]
    nb = n // BLOCK
    span = BLOCK + 2 * WINDOW
    scale = HEAD_DIM ** -0.5
    kp = jnp.pad(k, ((0, 0), (WINDOW, WINDOW), (0, 0), (0, 0)))
    vp = jnp.pad(v, ((0, 0), (WINDOW, WINDOW), (0, 0), (0, 0)))
    qb = q.reshape(b, nb, BLOCK, N_KV_HEADS, Q_GROUP, HEAD_DIM).transpose(1, 0, 2, 3, 4, 5)

    def one(args):
        j, qblk = args
        start = j * BLOCK
        kw = lax.dynamic_slice_in_dim(kp, start, span, axis=1)
        vw = lax.dynamic_slice_in_dim(vp, start, span, axis=1)
        qpos = start + jnp.arange(BLOCK)
        kpos = start - WINDOW + jnp.arange(span)
        valid = (jnp.abs(qpos[:, None] - kpos[None, :]) <= WINDOW) & (kpos >= 0)[None, :] & (kpos < n)[None, :]
        s_loc = jnp.einsum('bqkgd,bskd->bkgqs', qblk, kw).astype(jnp.float32) * scale
        s_loc = jnp.where(valid[None, None, None], s_loc, NEG)
        s_ctx = jnp.einsum('bqkgd,bskd->bkgqs', qblk, ck).astype(jnp.float32) * scale
        sc = jnp.concatenate([s_loc, s_ctx], axis=-1)
        vals = jnp.concatenate([vw, cv], axis=1)
        return sink_softmax_av(sc, vals, sink)

    out = lax.map(one, (jnp.arange(nb), qb))
    return out.transpose(1, 0, 2, 3, 4, 5).reshape(b, n, ATTN_WIDTH)

def expert_choice_ffn(h, w_r, b_r, w_g, w_u, w_d):
    shp = h.shape
    xt = h.reshape(-1, D_MODEL)
    n = xt.shape[0]
    cap = EC_FACTOR * n // N_EXPERTS
    logits = (xt @ w_r).astype(jnp.float32) + b_r.astype(jnp.float32)
    aff = jax.nn.softmax(logits, axis=-1)
    gate, idx = lax.top_k(aff.T, cap)
    xe = xt[idx]
    hid = jax.nn.silu(jnp.einsum('ecd,edf->ecf', xe, w_g)) * jnp.einsum('ecd,edf->ecf', xe, w_u)
    ye = jnp.einsum('ecf,efd->ecd', hid, w_d) * gate[..., None].astype(xe.dtype)
    out = jnp.zeros_like(xt).at[idx.reshape(-1)].add(ye.reshape(-1, D_MODEL))
    return out.reshape(shp)

def trunk_layer(x, mod, n1g, w_in, conv_dw, conv_dw_b, conv_ln_g, conv_ln_b, w_conv_out,
                sink, w_attn_out, w_out, n2g, w_router, b_router, w_eg, w_eu, w_ed,
                ctx_k=None, ctx_v=None):
    sh1, sc1, g1, sh2, sc2, g2 = mod
    b, n, _ = x.shape
    h = rmsnorm(x, n1g) * (1 + sc1) + sh1
    u = h @ w_in
    glu_in, q, k, v, ga, gb = jnp.split(u, SPLITS, axis=-1)
    conv_out = conformer_conv(glu_in, conv_dw, conv_dw_b, conv_ln_g, conv_ln_b, w_conv_out)
    q = q.reshape(b, n, N_HEADS, HEAD_DIM)
    k = k.reshape(b, n, N_KV_HEADS, HEAD_DIM)
    v = v.reshape(b, n, N_KV_HEADS, HEAD_DIM)
    if ctx_k is None:
        att = context_attention(q, k, v, sink)
    else:
        att = latent_attention(rope_2d(q), rope_2d(k), v, ctx_k, ctx_v, sink)
    attn_out = att @ w_attn_out
    mixed = (jax.nn.sigmoid(ga) * conv_out + jax.nn.sigmoid(gb) * attn_out) @ w_out
    x = x + g1 * mixed
    h2 = rmsnorm(x, n2g) * (1 + sc2) + sh2
    x = x + g2 * expert_choice_ffn(h2, w_router, b_router, w_eg, w_eu, w_ed)
    return x, k, v

def setup_inputs(seed: int = 0) -> dict:
    key = jax.random.key(seed)
    ks = jax.random.split(key, 32)
    f32 = jnp.float32
    nrm = lambda k, shp, s: jax.random.normal(k, shp, f32) * s
    D = D_MODEL
    return {
        "x_prompt": nrm(ks[0], (BATCH, SEQ, D), 1.0),
        "x_sample": nrm(ks[1], (DEC_BATCH, DEC_SEQ, D), 1.0),
        "c": nrm(ks[2], (DEC_BATCH, D), 1.0),
        "cache_k": nrm(ks[3], (DEC_BATCH, DEPTH, PAST_LEN, N_KV_HEADS, HEAD_DIM), 1.0),
        "cache_v": nrm(ks[4], (DEC_BATCH, DEPTH, PAST_LEN, N_KV_HEADS, HEAD_DIM), 1.0),
        "c_ctx": nrm(ks[5], (D,), 1.0),
        "w_ada": nrm(ks[6], (DEPTH, D, N_MOD * D), 0.5 * D ** -0.5),
        "b_ada": nrm(ks[7], (DEPTH, N_MOD * D), 0.01),
        "norm1_g": 1.0 + nrm(ks[8], (DEPTH, D), 0.01),
        "w_in": nrm(ks[9], (DEPTH, D, IN_COLS), D ** -0.5),
        "conv_dw": nrm(ks[10], (DEPTH, CONV_KERNEL, CONV_WIDTH), CONV_KERNEL ** -0.5),
        "conv_dw_b": nrm(ks[11], (DEPTH, CONV_WIDTH), 0.01),
        "conv_ln_g": 1.0 + nrm(ks[12], (DEPTH, CONV_WIDTH), 0.01),
        "conv_ln_b": nrm(ks[13], (DEPTH, CONV_WIDTH), 0.01),
        "w_conv_out": nrm(ks[14], (DEPTH, CONV_WIDTH, D), CONV_WIDTH ** -0.5),
        "attn_sink": nrm(ks[15], (DEPTH, N_HEADS), 0.5),
        "w_attn_out": nrm(ks[16], (DEPTH, ATTN_WIDTH, D), ATTN_WIDTH ** -0.5),
        "w_out": nrm(ks[17], (DEPTH, D, D), D ** -0.5),
        "norm2_g": 1.0 + nrm(ks[18], (DEPTH, D), 0.01),
        "w_router": nrm(ks[19], (DEPTH, D, N_EXPERTS), D ** -0.5),
        "b_router": nrm(ks[20], (DEPTH, N_EXPERTS), 0.01),
        "w_exp_gate": nrm(ks[21], (DEPTH, N_EXPERTS, D, D_EXPERT), D ** -0.5),
        "w_exp_up": nrm(ks[22], (DEPTH, N_EXPERTS, D, D_EXPERT), D ** -0.5),
        "w_exp_down": nrm(ks[23], (DEPTH, N_EXPERTS, D_EXPERT, D), D_EXPERT ** -0.5),
        "final_norm_g": 1.0 + nrm(ks[24], (D,), 0.01),
    }

def reference(x_prompt, x_sample, c, cache_k, cache_v, c_ctx, w_ada, b_ada, norm1_g, w_in,
              conv_dw, conv_dw_b, conv_ln_g, conv_ln_b, w_conv_out, attn_sink, w_attn_out,
              w_out, norm2_g, w_router, b_router, w_exp_gate, w_exp_up, w_exp_down,
              final_norm_g):
    xp = x_prompt
    xs = x_sample
    new_k = []
    new_v = []
    for l in range(DEPTH):
        lp = (norm1_g[l], w_in[l], conv_dw[l], conv_dw_b[l], conv_ln_g[l], conv_ln_b[l],
              w_conv_out[l], attn_sink[l], w_attn_out[l], w_out[l], norm2_g[l],
              w_router[l], b_router[l], w_exp_gate[l], w_exp_up[l], w_exp_down[l])
        mod_ctx = modulate_params(c_ctx[None, :], w_ada[l], b_ada[l])
        mod_lat = modulate_params(c, w_ada[l], b_ada[l])
        xp, k_ctx, v_ctx = trunk_layer(xp, mod_ctx, *lp)
        new_k.append(k_ctx)
        new_v.append(v_ctx)
        xs, _, _ = trunk_layer(xs, mod_lat, *lp, ctx_k=cache_k[:, l], ctx_v=cache_v[:, l])
    state_k = jnp.stack(new_k, axis=1)
    state_v = jnp.stack(new_v, axis=1)
    y_prompt = rmsnorm(xp, final_norm_g)
    y_sample = rmsnorm(xs, final_norm_g)
    return (y_prompt, y_sample, state_k, state_v)


_drawn_inputs = setup_inputs


def setup_inputs(seed=0):
    import zlib

    import numpy as np

    out = dict(_drawn_inputs(seed))
    spreads = {}
    factors = {'cache_k': 6.151,
     'cache_v': 5.115,
     'b_ada': 4.327,
     'norm1_g': 5.971,
     'conv_dw_b': 8.0,
     'conv_ln_g': 8.0,
     'conv_ln_b': 8.0,
     'attn_sink': 8.0,
     'norm2_g': 8.0,
     'b_router': 8.0,
     'final_norm_g': 5.661}
    for name, (base, spread) in spreads.items():
        noise = np.random.default_rng([zlib.crc32(name.encode()), seed]).standard_normal(out[name].shape)
        drawn = base * np.exp(spread * noise) if base else spread * noise
        out[name] = __import__('jax').numpy.asarray(drawn.astype(out[name].dtype))
    for name, factor in factors.items():
        out[name] = (out[name] * factor).astype(out[name].dtype)
    return out
```

```python
import concourse.bass as bass
from concourse import mybir
from concourse.alu_op_type import AluOpType as ALU

F32 = mybir.dt.float32
F32R = mybir.dt.float32r
ACT = mybir.ActivationFunctionType
AX = mybir.AxisListType.X
ds = bass.ds

D = 2048
KT = D // 128
NL = 512
NC = 128
N = NL + NC
PAST = 256
NH, NKV, HD = 16, 4, 128
GROUP = NH // NKV
CW = D // 2
CT = CW // 128
TAPS = 31
PAD = TAPS // 2
NE = 16
FT = (D // 2) // 128
CAPL, CAPC = 2 * NL // NE, 2 * NC // NE
CAP = CAPL + CAPC
EPS = 1e-6
SCALE = HD ** -0.5
NEG = -1e30
HALF = N // 2
ZW = PAD + NL + 2 * PAD + NC + PAD
CO = ZW - 2 * PAD
UNIT = 2048

RAW, SPL = 4, 2
A1, QN, GN, SN, TN, CN, ON = 2 * KT, 24, 16, 32, 16, 8, 16
ADA = 6 * KT
U = 4
US = 8
G_Q = A1
G_G = G_Q + QN
G_S = G_G + GN
G_T = G_S + 3 * SN
G_C = G_T + TN
G_O = G_C + CN
G_E = G_O + ON
CREDIT = SPL


def raw_use(first, stride, body, i, k):
    at = first + stride * k
    return at % RAW, at // RAW + i * (body * stride // RAW)


def build(nc, a, out):
    def sem(name):
        return nc.alloc_semaphore(name)

    base = 16512
    X0 = base
    R0 = X0 + 2 * KT * N * 4
    S0 = R0 + RAW * UNIT * 4
    Y0 = S0 + 2 * SPL * UNIT * 4
    Z0 = 229344

    names = {}

    def at(name, shape, dtype, offset):
        offset = (offset + 31) // 32 * 32
        names[name] = nc.alloc_sbuf_tensor_at(name, shape, dtype, offset=offset)
        size = 4
        for x in shape[1:]:
            size *= x
        assert offset + size <= Z0, (name, offset + size)
        return names[name], offset + size

    hhi, o = at("hhi", [128, KT, N], F32R, X0)
    hlo, o = at("hlo", [128, KT, N], F32R, o)
    raw, o = at("raw", [128, RAW, UNIT], F32, R0)
    whi, o = at("whi", [128, SPL, UNIT], F32R, S0)
    wlo, o = at("wlo", [128, SPL, UNIT], F32R, o)

    o = Z0 - 4800
    SMALL = o
    mod, o = at("mod", [128, ADA, 2], F32, o)
    bada, o = at("bada", [128, ADA], F32, o)
    cond, o = at("cond", [128, KT, 2], F32, o)
    norms, o = at("norms", [128, 3, KT, 2], F32, o)
    gsc, o = at("gsc", [128, KT, 2], F32, o)
    ghalf, o = at("ghalf", [128, KT, 2], F32, o)
    taps, o = at("taps", [128, CT, TAPS], F32, o)
    convp, o = at("convp", [128, 3, CT], F32, o)
    sinks, o = at("sinks", [128, NH], F32, o)
    negsink, o = at("negsink", [128, NH], F32, o)
    ident, o = at("ident", [128, 128], F32, o)
    ones, o = at("ones", [128, 128], F32, o)
    mx, o = at("mx", [128, 2], F32, o)
    nm, o = at("nm", [128, 1], F32, o)
    dn, o = at("dn", [128, 3], F32, o)
    rd, o = at("rd", [128, 2], F32, o)
    brt, o = at("brt", [16, 1], F32, o)
    gates, o = at("gates", [128, 4], F32, o)

    xin, o = at("xin", [128, KT, N], F32, Y0)
    t1, o = at("t1", [128, N], F32, o)
    t2, o = at("t2", [128, N], F32, o)
    t3, o = at("t3", [128, N], F32, o)
    t4, o = at("t4", [128, N], F32, o)
    rstd, o = at("rstd", [128, N], F32, o)
    assert o <= SMALL

    zt, o = at("zt", [128, CT, ZW], F32, Y0)
    ctmp, o = at("ctmp", [128, CO], F32, o)
    ktg, o = at("ktg", [128, N + PAST], F32, o)
    vg, o = at("vg", [128, (N + PAST) // 128, HD], F32, o)
    qh, o = at("qh", [128, 2, N], F32, o)
    sm, o = at("sm", [128, 384], F32, o)
    pe_, o = at("pexp", [128, 640], F32, o)
    pn, o = at("pn", [128, 640], F32, o)
    pt_sb, o = at("pt_sb", [128, 640], F32, o)
    ao, o = at("ao", [128, 2, 128], F32, o)
    th, o = at("th", [128, 2, N], F32, o)
    mask, o = at("mask", [128, 384], F32, o)
    assert o <= SMALL, (o, SMALL)
    cost, o = at("cost", [128, N], F32, Y0)
    sint, o = at("sint", [128, N], F32, o)
    ra, o = at("ra", [128, N], F32, o)
    rb, o = at("rb", [128, N], F32, o)
    rbs, o = at("rbs", [128, N], F32, o)
    ro, o = at("ro", [128, N], F32, o)
    vst, o = at("vst", [128, N], F32, o)
    vtk, o = at("vtk", [128, N], F32, o)
    assert o <= Y0 + CT * ZW * 4
    gsig, o = at("gsig", [128, N], F32, Y0 + CT * ZW * 4)

    alo, o = at("alo", [128, CT, N], F32R, Y0)
    ahi, o = at("ahi", [128, CT, N], F32R, Y0 + CT * ZW * 4)
    gl, o = at("gl", [128, 2, N], F32, o)
    att4, _ = at("att4", [128, 4, N], F32, o - 2 * N * 4)
    mo, o = at("mo", [128, 2, N], F32, o)
    lt1, o = at("lt1", [128, N], F32, o)
    lt2, o = at("lt2", [128, N], F32, o)
    assert o <= SMALL, (o, SMALL)
    ls1, _ = at("ls1", [128, 672], F32, Y0 + CT * ZW * 4)
    ls2, _ = at("ls2", [128, 672], F32, Y0 + CT * ZW * 4 + 2688)
    ls3, _ = at("ls3", [128, 672], F32, Y0 + CT * ZW * 4 + 2 * 2688)
    lq, _ = at("lq", [128, 2, 672], F32, Y0 + CT * ZW * 4 + 3 * 2688)

    xr, o = at("xr", [128, KT, N], F32, Y0)
    YE = o
    sq, o = at("sq", [128, N], F32, YE)
    ssum, o = at("ssum", [128, N], F32, o)
    e1, o = at("e1", [128, N], F32, o)
    e2, o = at("e2", [128, N], F32, o)
    e3, o = at("e3", [128, N], F32, o)
    h2t, o = at("h2t", [128, 1, N], F32, o)
    assert o <= SMALL, (o, SMALL)
    h2hi, o = at("h2hi", [128, 5, D], F32R, X0)
    h2lo, o = at("h2lo", [128, 5, D], F32R, o)
    xe, o = at("xe", [128, KT, CAP], F32, S0)
    hid, o = at("hid", [128, FT, CAP], F32, o)
    yt, o = at("yt", [128, KT, 128], F32, o)
    yhi, o = at("yhi", [128, 2, 512], F32R, o)
    ylo, o = at("ylo", [128, 2, 512], F32R, o)
    sl, o = at("sl", [128, 4, 128], F32R, o)
    sc, o = at("sc", [128, 32], F32R, o)
    sg, o = at("sg", [128, 4, 128], F32, o)
    stt_, o = at("stt", [128, 512], F32R, o)
    sil, o = at("sil", [128, 2, CAP], F32, o)
    sgx, o = at("sgx", [128, NE * CAPC], F32, o)
    assert o <= Y0, (o, Y0)
    ytc, _ = at("ytc", [128, KT, NE * CAPC], F32, YE)
    wr, _ = at("wr", [128, KT, NE], F32, S0)
    lgT, o = at("lgT", [16, N], F32, S0 + 1024)
    work, o = at("work", [16, N], F32, o)
    affT, o = at("affT", [16, N], F32, o)
    top8, o = at("top8", [16, 8], F32, o)
    sm5, o = at("sm5", [128, 5, NE], F32, o)
    sm5b, o = at("sm5b", [128, 5], F32, o)
    trio, o = at("trio", [128, 2, 128], F32, o)
    mk5, o = at("mk5", [128, 5, NE], F32, o)
    PW = YE + KT * NE * CAPC * 4
    aff, o = at("aff", [128, 5, NE + 2], F32, PW)
    posm, o = at("posm", [128, 5, NE + 2], F32, o)
    iota, o = at("iota", [128, 64], F32, o)
    scx, o = at("scx", [128, NE * CAPC], F32R, o)
    stx, o = at("stx", [128, 2, 128], F32R, o)
    assert o <= SMALL, (o, SMALL)

    pu = nc.alloc_psum_tensor("pu", [128, 4, 512], F32)
    ps = nc.alloc_psum_tensor("ps", [128, 2, 512], F32)
    pt = nc.alloc_psum_tensor("pt", [128, 2, 512], F32)

    def dr(name, shape):
        return nc.dram_tensor(name, shape, F32).ap()

    qT_d, kT_d = dr("q_rot", [NH, 128, N]), dr("k_rot", [NKV, 128, N])
    v_d = dr("v_tok", [NKV, 128, 5, HD])
    at_d = dr("att", [NH, 128, N])
    th_d = dr("gates_tanh", [2 * KT, 128, N])
    mx_d = dr("mixed_a", [KT, 128, N])

    raw_loaded = [sem(f"raw_loaded{i}") for i in range(RAW)]
    raw_freed = [sem(f"raw_freed{i}") for i in range(RAW)]
    hi_ready, lo_ready = sem("hi_ready"), sem("lo_ready")
    dense_mm = sem("dense_mm")
    psum_free = [sem("psum_free0"), sem("psum_free1")]
    ada_read = sem("ada_read")
    small_loaded = sem("small_loaded")
    x_loaded = [sem(f"x_loaded{i}") for i in range(4)]
    const_made = sem("const_made")
    cond_ready = sem("cond_ready")
    sq_made, sq_summed = sem("sq_made"), sem("sq_summed")
    norm_mm, norm_t, norm_sq = sem("norm_mm"), sem("norm_t"), sem("norm_sqrt")
    vec_done = sem("vec_done")
    act_done = sem("act_done")
    gsc_ready = sem("gsc_ready")
    xn_ready = sem("xn_ready")
    h_hi, h_lo = sem("h_hi"), sem("h_lo")
    tabs_loaded = sem("tabs_loaded")
    rope_b, rope_swapped, rope_out, rope_stored = sem("rope_b"), sem("rope_swapped"), sem("rope_out"), sem("rope_stored")
    rope_a = sem("rope_a")
    v_read, v_tr, v_tok, v_stored, vx_stored = sem("v_read"), sem("v_tr"), sem("v_tok"), sem("v_stored"), sem("vx_stored")
    glu_sig, glu_z = sem("glu_sig"), sem("glu_z")
    z_zero = sem("z_zero")
    kv_loaded, q_loaded = sem("kv_loaded"), [sem("q_loaded0"), sem("q_loaded1")]
    att_qk, att_nm, att_exp, att_pn = sem("att_qk"), sem("att_nm"), sem("att_exp"), sem("att_pn")
    att_tr, att_pt, att_pv, att_out = sem("att_tr"), sem("att_pt"), sem("att_pv"), sem("att_out")
    att_v = sem("att_v")
    att_stored = [sem("att_stored0"), sem("att_stored1")]
    conv_done = sem("conv_done")
    th_ready, th_stored = sem("th_ready"), [sem("th_stored0"), sem("th_stored1")]
    attn_loaded, attn_hi, attn_lo = [sem(f"attn_loaded{i}") for i in range(4)], sem("attn_hi"), sem("attn_lo")
    gl_loaded = [sem("gl_loaded0"), sem("gl_loaded1")]
    mo_ready, mo_stored = sem("mo_ready"), [sem("mo_stored0"), sem("mo_stored1")]
    ln_sum, ln_mm, ln_sq, ln_c = sem("ln_sum"), sem("ln_mm"), sem("ln_sq"), sem("ln_c")
    ln_act, ln_hi, ln_lo = sem("ln_act"), sem("ln_hi"), sem("ln_lo")
    ml_loaded = [sem("ml_loaded0"), sem("ml_loaded1")]
    mix_sum, mix_hi, mix_lo = sem("mix_sum"), sem("mix_hi"), sem("mix_lo")
    xr_loaded = sem("xr_loaded")
    res_done, res_sq, res_sum = sem("res_done"), sem("res_sq"), sem("res_sum")
    h2_vec, h2_act, h2_tr, h2_hi, h2_lo, h2_mm = (sem("h2_vec"), sem("h2_act"), sem("h2_tr"), sem("h2_hi"),
                                                  sem("h2_lo"), sem("h2_mm"))
    rt_loaded = sem("rt_loaded")
    rt_pe, rt_vec, rt_act = sem("rt_pe"), sem("rt_vec"), sem("rt_act")
    sel_made, sel_st, st_read = sem("sel_made"), sem("sel_st"), sem("st_read")
    ga_mm, ga_read = sem("ga_mm"), sem("ga_read")
    gu_mm, gu_sil, gu_hid = sem("gu_mm"), sem("gu_sil"), sem("gu_hid")
    dn_mm, dn_read = sem("dn_mm"), sem("dn_read")
    tr_mm, tr_hi, tr_lo = sem("tr_mm"), sem("tr_hi"), sem("tr_lo")
    sc_mm, sc_add = sem("sc_mm"), sem("sc_add")
    fin_sq, fin_sum, fin_mm, fin_c, fin_y, fin_stored = (sem("fin_sq"), sem("fin_sum"), sem("fin_mm"), sem("fin_c"),
                                                         sem("fin_y"), sem("fin_stored"))
    states_stored = sem("states_stored")
    pool_passed, vec_passed = sem("pool_passed"), sem("vec_passed")

    SEGS = [(0, 0, 0, HALF), (HALF, 1, 0, NL - HALF), (NL, 1, NL - HALF, HALF)]

    def att_steps():
        return [(h, j) for h in range(GROUP) for j in range(NL // 128 + 1)]

    STEPS = att_steps()
    NS = len(STEPS)
    CUT = [NS * k // US for k in range(US + 1)]

    def keys_of(j):
        lo, hi = max(0, j - 1), min(NL // 128, j + 2)
        return lo, hi

    def sync_program(sp):
        def load(src, slot, use, first=False):
            if not first:
                sp.wait_ge(raw_freed[slot], 2 * use)
            sp.dma_start(raw[:, slot, :], src).then_inc(raw_loaded[slot], 16)

        for k in range(RAW):
            load(a["w_ada"][k], k, 0, first=True)
        with sp.Fori(1, A1 // RAW) as i:
            for k in range(RAW):
                load(a["w_ada"][i * RAW + k], *raw_use(0, 1, RAW, i, k))
        with sp.Fori(0, (QN + GN) // U) as i:
            for k in range(U):
                load(a["w_in"][i * U + k], *raw_use(G_Q, 1, U, i, k))
        with sp.Fori(0, SN // US) as i:
            for k in range(US):
                slot, use = raw_use(G_S, 3, US, i, k)
                load(a["w_in"][i * US + (QN + GN + k)], slot, use)
                for b in range(2):
                    at_ = G_S + 3 * k + 1 + b
                    load(a["w_ada"][i * (2 * US) + (A1 + 2 * k + b)], at_ % RAW, at_ // RAW + i * (3 * US // RAW))
        for name, first, n in (("w_attn_out", G_T, TN), ("w_conv_out", G_C, CN), ("w_out", G_O, ON)):
            with sp.Fori(0, n // U) as i:
                for k in range(U):
                    load(a[name][i * U + k], *raw_use(first, 1, U, i, k))
        per = 3 * FT
        with sp.Fori(0, NE) as e:
            for k in range(2 * FT):
                load(a["w_gu"][e * (2 * FT) + k], *raw_use(G_E, 1, per, e, k))
            for k in range(FT):
                load(a["w_exp_down"][e * FT + k], *raw_use(G_E, 1, per, e, 2 * FT + k))

    def pool_program(pool):
        def settle():
            pool.sem_inc(pool_passed, 1)

        pool.memset(ident[:, :], 0.0).then_inc(const_made, 1)
        pool.memset(ones[:, :], 1.0 / D).then_inc(const_made, 1)
        pool.wait_ge(const_made, 2)
        pool.affine_select(out=ident[:, :], in_=ident[:, :], compare_op=ALU.not_equal, fill=1.0, base=0,
                           pattern=[[-1, 128]], channel_multiplier=1).then_inc(const_made, 1)
        for dst, name in ((cond, "cond"), (bada, "b_ada"), (norms, "norms"), (taps, "taps"), (convp, "convp"),
                          (sinks, "sinks")):
            pool.dma_start(dst[:], a[name]).then_inc(small_loaded, 16)
        pool.dma_start(brt[:, :], a["b_router"]).then_inc(small_loaded, 16)
        for c in range(4):
            pool.dma_start(xin[:, 4 * c:4 * c + 4, :], a["x"][:, 4 * c:4 * c + 4, :]).then_inc(x_loaded[c], 16)
        pool.wait_ge(h_lo, KT)
        pool.dma_start(cost[:, :], a["cos"]).then_inc(tabs_loaded, 16)
        pool.dma_start(sint[:, :], a["sin"]).then_inc(tabs_loaded, 16)
        pool.dma_start(mask[:, :], a["mask"]).then_inc(tabs_loaded, 16)

        def store_v(n):
            pool.wait_ge(v_read, n + 1)
            pool.dma_start(out["v"][n], vst[:, NL:N]).then_inc(vx_stored, 16)
            pool.wait_ge(v_tok, n + 1)
            pool.dma_start(v_d[n], vtk[:, :].rearrange("p (t d) -> p t d", d=HD)).then_inc(v_stored, 16)

        def rotate(n, dst, state=None):
            pool.wait_ge(rope_b, n + 1)
            settle()
            for q in range(4):
                s = q ^ 1
                pool.dma_start(rbs[32 * q:32 * q + 32, :], rb[32 * s:32 * s + 32, :]).then_inc(rope_swapped, 16)
            pool.wait_ge(rope_out, n + 1)
            settle()
            pool.dma_start(dst, ro[:, :]).then_inc(rope_stored, 16)
            if state is not None:
                pool.dma_start(state, ro[:, NL:N]).then_inc(rope_stored, 16)

        for n in range(NKV):
            store_v(n)
        for n in range(NKV):
            rotate(n, kT_d[n], out["k"][n])
        with pool.Fori(0, NH) as n:
            rotate(n + NKV, qT_d[n])

        def load_group(i):
            pool.wait_ge(rope_stored, 16 * (2 * NKV + NH))
            pool.wait_ge(v_stored, 16 * NKV)
            pool.wait_ge(att_pv, NS * i)
            settle()
            pool.dma_start(ktg[:, 0:N], kT_d[i]).then_inc(kv_loaded, 16)
            pool.dma_start(ktg[:, N:N + PAST], a["cache_k"][i]).then_inc(kv_loaded, 16)
            pool.dma_start(vg[:, 0:5, :], v_d[i]).then_inc(kv_loaded, 16)
            pool.dma_start(vg[:, 5:7, :], a["cache_v"][i]).then_inc(kv_loaded, 16)

        def load_q(i, h):
            pool.wait_ge(att_qk, NS * i + 5 * h + 5)
            settle()
            pool.dma_start(qh[:, h % 2, :], qT_d[i * GROUP + h]).then_inc(q_loaded[h % 2], 16)

        with pool.Fori(0, NKV) as i:
            load_group(i)
            load_q(i, 0)
            load_q(i, 1)
            for k in range(US):
                for n in range(CUT[k], CUT[k + 1]):
                    h, j = STEPS[n]
                    if j == 0 and 0 < h and h + 1 < GROUP:
                        load_q(i, h + 1)
                    pool.wait_ge(att_out, i * NS + (n + 1))
                    settle()
                    pool.dma_start(at_d[i * GROUP + h][:, 128 * j:128 * j + 128],
                                   ao[:, n % 2, :]).then_inc(att_stored[n % 2], 16)
                pool.wait_ge(th_ready, i * US + (k + 1))
                settle()
                pool.dma_start(th_d[i * US + k], th[:, k % 2, :]).then_inc(th_stored[k % 2], 16)

        for b in range(2):
            pool.wait_ge(att_stored[b], 16 * (NKV * NS // 2))
            pool.wait_ge(th_stored[b], 16 * (SN // 2))

        def gate_load(m, which):
            pool.dma_start(gl[:, m % 2, :], th_d[which * KT + m]).then_inc(gl_loaded[m % 2], 16)

        for m in range(KT):
            if m >= 4:
                pool.wait_ge(attn_lo, m - 3)
            pool.dma_start(att4[:, m % 4, :], at_d[m]).then_inc(attn_loaded[m % 4], 16)
        pool.wait_ge(attn_lo, KT)
        for m in range(2):
            gate_load(m, 1)
        for m in range(KT):
            pool.wait_ge(mo_ready, m + 1)
            pool.dma_start(mx_d[m], mo[:, m % 2, :]).then_inc(mo_stored[m % 2], 16)
            if m + 2 < KT:
                gate_load(m + 2, 1)
        for b in range(2):
            pool.wait_ge(mo_stored[b], 16 * (KT // 2))
        for m in range(KT):
            if m >= 2:
                pool.wait_ge(mix_sum, m - 1)
            gate_load(m, 0)
            pool.dma_start(mo[:, m % 2, :], mx_d[m]).then_inc(ml_loaded[m % 2], 16)
        pool.wait_ge(dense_mm, CREDIT + QN + GN + SN + TN + 2 * CN)
        for c in range(4):
            pool.dma_start(xr[:, 4 * c:4 * c + 4, :], a["x"][:, 4 * c:4 * c + 4, :]).then_inc(xr_loaded, 16)
        pool.wait_ge(dense_mm, CREDIT + QN + GN + SN + TN + 2 * CN + ON)
        pool.dma_start(wr[:, :, :], a["w_router"]).then_inc(rt_loaded, 16)
        pool.dma_start(trio[:, :, :], a["triangle"]).then_inc(rt_loaded, 16)
        pool.dma_start(iota[:, :], a["iota"]).then_inc(rt_loaded, 16)
        with pool.Fori(0, KT) as m:
            pool.wait_ge(fin_y, m + 1)
            settle()
            pool.dma_start(out["y"][m], xr[:, ds(m, 1), :].rearrange("p a n -> p (a n)")).then_inc(fin_stored, 16)
        pool.wait_ge(fin_stored, 16 * KT)
        pool.wait_ge(vx_stored, 16 * NKV)
        pool.wait_ge(rope_stored, 16 * (2 * NKV + NH))

    def norm_chain(vec, act_side, step, total, mean, t, r, w1, w2, width):
        n = total

        def did(ins):
            nonlocal n
            ins.then_inc(step, 1)
            n += 1
            vec.wait_ge(step, n)

        did(nc.vector.tensor_scalar(t, mean, EPS, None, ALU.add))
        did(nc.vector.reciprocal(w1, t))
        act_side(n)
        did(nc.vector.tensor_tensor(w2, r, r, ALU.mult))
        did(nc.vector.tensor_tensor(w2, w2, t, ALU.mult))
        did(nc.vector.tensor_scalar(w2, w2, -0.5, 1.5, ALU.mult, ALU.add))
        did(nc.vector.tensor_tensor(r, r, w2, ALU.mult))
        return n

    def tensor_program(pe):
        def ada_unit(slot, use, read, bank):
            pe.wait_ge(raw_loaded[slot], 16 * (use + 1))
            pe.wait_ge(ada_read, read)
            for kt in range(KT):
                last = nc.tensor.matmul(bank[:, 0:2], raw[:, slot, kt * 128:kt * 128 + 128], cond[:, kt, :],
                                        start=kt == 0, stop=kt == KT - 1)
            last.then_inc(raw_freed[slot], 2)

        def dense(d, p, dk, pk, hi, lo, k0, k1, off, kts):
            for kt in range(k0, k1):
                w = off + kt * 128
                for c in range(2):
                    o = pu[:, 2 * pk + c, 0:HALF]
                    cols = slice(c * HALF, c * HALF + HALF)
                    nc.tensor.matmul(o, whi[:, dk, w:w + 128], hi[:, kt, cols], start=kt == 0, stop=False)
                    nc.tensor.matmul(o, whi[:, dk, w:w + 128], lo[:, kt, cols], start=False, stop=False)
                    last = nc.tensor.matmul(o, wlo[:, dk, w:w + 128], hi[:, kt, cols], start=False,
                                            stop=kt == kts - 1)
            if k1 == kts:
                last.then_inc(dense_mm, 1)

        def dense_start(d, p, i=0, body=0):
            pe.wait_ge(hi_ready, d + 1)
            pe.wait_ge(lo_ready, d + 1)
            pe.wait_ge(psum_free[p % 2], i * (body // 2) + (p // 2 + 1))

        def mean_over_channels(src, dst, width, signal):
            for c in range(2):
                last = nc.tensor.matmul(dst[:, c, 0:width], ones[:, :], src[:, c * width:(c + 1) * width],
                                        start=True, stop=True)
            last.then_inc(signal, 1)

        pe.sem_inc(dense_mm, CREDIT)
        pe.sem_inc(att_qk, 10)
        pe.wait_ge(const_made, 3)
        pe.wait_ge(cond_ready, 1)
        with pe.Fori(0, A1 // RAW) as i:
            for k in range(RAW):
                ada_unit(*raw_use(0, 1, RAW, i, k), i * RAW + k + 1, pu[:, k, :])
        pe.wait_ge(sq_summed, KT)
        pe.wait_ge(ada_read, RAW + A1)
        mean_over_channels(t1, pu, HALF, norm_mm)
        pe.wait_ge(h_hi, KT)
        pe.wait_ge(h_lo, KT)
        for d in range(2 * NKV):
            dense_start(d, d)
            dense(d, d, d % 2, d % 2, hhi, hlo, 0, KT, 0, KT)
            if 1 <= d <= NKV:
                n = d - 1
                pe.wait_ge(v_read, n + 1)
                if n:
                    pe.wait_ge(v_tok, n)
                for t in range(5):
                    last = nc.tensor.transpose(pt[:, t // 4, 128 * (t % 4):128 * (t % 4) + 128],
                                               vst[:, 128 * t:128 * t + 128], ident[:, :])
                last.then_inc(v_tr, 1)
        with pe.Fori(2 * NKV // U, (QN + GN) // U) as i:
            for k in range(U):
                d = i * U + k
                dense_start(d, k, i, U)
                dense(d, d, k % 2, k % 2, hhi, hlo, 0, KT, 0, KT)

        def qk(i, n):
            h, j = STEPS[n]
            if n == 0:
                pe.wait_ge(kv_loaded, i * 64 + 64)
            if j == 0:
                uses = 2
                pe.wait_ge(q_loaded[h % 2], (i * uses + (h // 2 + 1)) * 16)
            pe.wait_ge(att_exp, i * NS + n)
            pe.wait_ge(att_pt, i * NS + n)
            qb = qh[:, h % 2, 128 * j:128 * j + 128]
            if j < NL // 128:
                lo, hi = keys_of(j)
                nc.tensor.matmul(ps[:, 0, 0:128 * (hi - lo)], qb, ktg[:, 128 * lo:128 * hi], start=True, stop=True)
                last = nc.tensor.matmul(ps[:, 1, 0:PAST], qb, ktg[:, N:N + PAST], start=True, stop=True)
            else:
                last = nc.tensor.matmul(ps[:, 0, 0:NC], qb, ktg[:, NL:N], start=True, stop=True)
            last.then_inc(att_qk, 1)

        def turn(i, n):
            h, j = STEPS[n]
            lo, hi = keys_of(j)
            blocks = hi - lo + 2 if j < 4 else 1
            pe.wait_ge(att_pn, i * NS + (n + 1))
            pe.wait_ge(att_out, i * NS + n)
            for b in range(blocks):
                last = nc.tensor.transpose(pt[:, 0, 128 * b:128 * b + 128] if b < 4 else ps[:, 1, 0:128],
                                           pn[:, 128 * b:128 * b + 128], ident[:, :])
            last.then_inc(att_tr, 1)

        def pv(i, n):
            h, j = STEPS[n]
            lo, hi = keys_of(j)
            vs = [*range(lo, hi), 5, 6] if j < 4 else [4]
            pe.wait_ge(att_pt, i * NS + (n + 1))
            for b, v in enumerate(vs):
                last = nc.tensor.matmul(pt[:, 0, 0:128], vg[:, v, :], pt_sb[:, 128 * b:128 * b + 128],
                                        start=b == 0, stop=b == len(vs) - 1)
            last.then_inc(att_pv, 1)

        with pe.Fori(0, SN // US) as i:
            for k in range(US):
                d = i * US + (QN + GN + k)
                dense_start(d, QN + GN + k, i, US)
                steps = list(range(CUT[k], CUT[k + 1]))
                cuts = [KT * x // len(steps) for x in range(len(steps) + 1)]
                for x, n in enumerate(steps):
                    qk(i, n)
                    dense(d, d, k % 2, k % 2, hhi, hlo, cuts[x], cuts[x + 1], 0, KT)
                    turn(i, n)
                    if x < 2:
                        at_ = G_S + 3 * k + 1 + x
                        ada_unit(at_ % RAW, at_ // RAW + i * (3 * US // RAW),
                                 i * (2 * US) + (RAW + A1 + 2 * k + x), pt[:, 1, :])
                    pv(i, n)

        D_T = QN + GN + SN
        for t in range(TN):
            d = D_T + t
            dense_start(d, d)
            for kt in range(KT):
                if t == 0:
                    pe.wait_ge(attn_hi, kt + 1)
                    pe.wait_ge(attn_lo, kt + 1)
                dense(d, d, t % 2, t % 2, hhi, hlo, kt, kt + 1, 0, KT)
            if t == 1:
                pe.wait_ge(ln_sum, 1)
                mean_over_channels(ls1, ps, CO // 2, ln_mm)
            if t == 3:
                pe.wait_ge(ln_sum, 2)
                mean_over_channels(ls1, pt, CO // 2, ln_mm)
        pe.wait_ge(ln_hi, CT)
        pe.wait_ge(ln_lo, CT)
        for c in range(CN):
            for b in range(2):
                d, p = D_T + TN + c, D_T + TN + 2 * c + b
                dense_start(d, p)
                dense(d, p, c % 2, b, ahi, alo, 0, CT, b * CT * 128, CT)
        pe.wait_ge(mix_hi, KT)
        pe.wait_ge(mix_lo, KT)
        with pe.Fori(0, ON // U) as i:
            for k in range(U):
                d = i * U + (D_T + TN + CN + k)
                p = D_T + TN + 2 * CN + k
                dense_start(d, p, i, U)
                dense(d, p, k % 2, k % 2, hhi, hlo, 0, KT, 0, KT)

        pe.wait_ge(res_sum, KT)
        mean_over_channels(ssum, ps, HALF, norm_mm)
        pe.wait_ge(rt_loaded, 48)
        for kt in range(KT):
            pe.wait_ge(h2_act, kt + 1)
            nc.tensor.matmul(ps[0:16, 0, :], wr[:, kt, :], h2t[:, 0, 0:NL], start=kt == 0, stop=kt == KT - 1)
            nc.tensor.matmul(ps[0:16, 1, 0:NC], wr[:, kt, :], h2t[:, 0, NL:N], start=kt == 0, stop=kt == KT - 1)
            if kt >= 2:
                pe.wait_ge(h2_hi, kt - 1)
                pe.wait_ge(h2_lo, kt - 1)
            for t in range(5):
                last = nc.tensor.transpose(pu[:, 2 * (kt % 2) + t // 4, 128 * (t % 4):128 * (t % 4) + 128],
                                           h2t[:, 0, 128 * t:128 * t + 128], ident[:, :])
            last.then_inc(h2_tr, 1)
        pe.wait_ge(rt_act, 1)
        for t in range(5):
            last = nc.tensor.transpose(pt[:, 0, NE * t:NE * t + NE], lgT[:, 128 * t:128 * t + 128],
                                       ident[0:16, 0:16])
        last.then_inc(rt_pe, 1)
        pe.wait_ge(rt_vec, RV_AFF)
        for t in range(5):
            last = nc.tensor.transpose(ps[0:16, t // 4, 128 * (t % 4):128 * (t % 4) + 128], aff[:, t, 0:NE],
                                       ident[:, :])
        last.then_inc(rt_pe, 1)
        pe.wait_ge(rt_vec, RV_MASK)
        for t in range(5):
            last = nc.tensor.transpose(pt[:, 0, NE * t:NE * t + NE], work[:, 128 * t:128 * t + 128],
                                       ident[0:16, 0:16])
        last.then_inc(rt_pe, 1)
        pe.wait_ge(rt_vec, RV_MK5)
        for t in range(5):
            first = 0 if t < 4 else 4
            for s in range(first, t + 1):
                last = nc.tensor.matmul(pt[:, 1, NE * t:NE * t + NE], trio[:, 0 if s == t else 1, :], mk5[:, s, :],
                                        start=s == first, stop=s == t)
        last.then_inc(rt_pe, 1)

        def gather(half, ready, n):
            pe.wait_ge(sel_made, ready)
            for kt in range(KT):
                b = kt // 4
                if kt % 4 == 0:
                    pe.wait_ge(ga_read, n * 4 + max(b - 1, 0))
                c = CAP * (kt % 4)
                o = ps[:, b % 2, c:c + CAPL]
                for t in range(4):
                    for x, part in enumerate((h2hi, h2lo)):
                        nc.tensor.matmul(o, part[:, t, kt * 128:kt * 128 + 128],
                                         sl[:, t, 64 * half:64 * half + 64], start=t == 0 and x == 0,
                                         stop=t == 3 and x == 1)
                for x, part in enumerate((h2hi, h2lo)):
                    last = nc.tensor.matmul(ps[:, b % 2, c + CAPL:c + CAP], part[:, 4, kt * 128:kt * 128 + 128],
                                            sc[:, 16 * half:16 * half + 16], start=x == 0, stop=x == 1)
                if kt % 4 == 3:
                    last.then_inc(ga_mm, 1)

        def gate_up(e, ek, n):
            pe.wait_ge(ga_read, (n + 1) * 4)
            for m in range(FT):
                for g in range(2):
                    k = 2 * m + g
                    slot, use = raw_use(G_E, 1, 3 * FT, e, k)
                    pe.wait_ge(raw_loaded[slot], 16 * (use + 1))
                    if m % 2 == 0 and g == 0:
                        b = m // 2
                        pe.wait_ge(gu_hid, n * 4 + max(b - 1, 0))
                    c = CAP * (2 * (m % 2) + g)
                    for kt in range(KT):
                        last = nc.tensor.matmul(pu[:, (m // 2) % 2, c:c + CAP],
                                                raw[:, slot, kt * 128:kt * 128 + 128], xe[:, kt, :],
                                                start=kt == 0, stop=kt == KT - 1)
                    last.then_inc(raw_freed[slot], 2)

        def down(e, n):
            pe.wait_ge(gu_hid, n * 4 + 4)
            for m in range(FT):
                slot, use = raw_use(G_E, 1, 3 * FT, e, 2 * FT + m)
                pe.wait_ge(raw_loaded[slot], 16 * (use + 1))
                pe.wait_ge(dn_read, n * FT + max(m - 1, 0))
                for b in range(2):
                    for f in range(FT):
                        last = nc.tensor.matmul(pu[:, 2 + m % 2, CAP * b:CAP * b + CAP],
                                                raw[:, slot, (b * FT + f) * 128:(b * FT + f) * 128 + 128],
                                                hid[:, f, :], start=f == 0, stop=f == FT - 1)
                last.then_inc(raw_freed[slot], 2)

        pe.wait_ge(rt_vec, RV_END)
        gather(0, 1, 0)
        with pe.Fori(0, NE // 2) as pair:
            pe.wait_ge(sc_add, pair * KT)
            for t in range(4):
                last = nc.tensor.transpose(pt[:, 0, 128 * t:128 * t + 128], sl[:, t, :].bitcast(F32), ident[:, :])
            for t in range(4):
                last = nc.tensor.matmul(pt[:, 1, 0:1], sg[:, t, :], ones[:, 0:1], start=t == 0, stop=t == 3)
            last.then_inc(sel_st, 1)
            for half in range(2):
                e = pair * 2 + half
                gate_up(e, half, e)
                if half == 0:
                    gather(1, pair * 1 + 1, e + 1)
                else:
                    gather(0, pair * 1 + 2, e + 1)
                down(e, e)
            pe.wait_ge(dn_read, pair * (2 * FT) + 2 * FT)
            pe.wait_ge(st_read, pair + 1)
            pe.wait_ge(ga_read, pair * 8 + 12)
            for q in range(KT // 4 + 1):
                if q < KT // 4:
                    if q >= 2:
                        pe.wait_ge(tr_lo, pair * 4 + (q - 1))
                        pe.wait_ge(tr_hi, pair * 4 + (q - 1))
                    for x in range(4):
                        last = nc.tensor.transpose(ps[:, q % 2, 128 * x:128 * x + 128], yt[:, 4 * q + x, :],
                                                   ident[:, :])
                    last.then_inc(tr_mm, 1)
                if q >= 1:
                    r = q - 1
                    pe.wait_ge(tr_lo, pair * 4 + (r + 1))
                    pe.wait_ge(tr_hi, pair * 4 + (r + 1))
                    for x in range(4):
                        m = 4 * r + x
                        pe.wait_ge(sc_add, pair * KT + max(m - 1, 0))
                        cols = slice(128 * x, 128 * x + 128)
                        nc.tensor.matmul(pt[:, m % 2, :], yhi[:, r % 2, cols], stt_[:, :], start=True, stop=False)
                        nc.tensor.matmul(pt[:, m % 2, :], ylo[:, r % 2, cols], stt_[:, :], start=False,
                                         stop=True).then_inc(sc_mm, 1)
        pe.wait_ge(sc_add, KT * (NE // 2))
        for hh in range(2):
            last = nc.tensor.transpose(pt[:, 0, 128 * hh:128 * hh + 128],
                                       scx[:, 128 * hh:128 * hh + 128].bitcast(F32), ident[:, :])
        for hh in range(2):
            last = nc.tensor.matmul(pt[:, 1, hh:hh + 1], sgx[:, 128 * hh:128 * hh + 128], ones[:, 0:1], start=True,
                                    stop=True)
        last.then_inc(sel_st, 1)
        pe.wait_ge(st_read, NE // 2 + 1)
        T0 = 4 * (NE // 2)
        for q in range(KT // 4):
            for hh in range(2):
                n = T0 + 2 * q + hh
                pe.wait_ge(tr_lo, n - 1)
                pe.wait_ge(tr_hi, n - 1)
                for x in range(4):
                    last = nc.tensor.transpose(ps[:, hh, 128 * x:128 * x + 128],
                                               ytc[:, 4 * q + x, 128 * hh:128 * hh + 128], ident[:, :])
                last.then_inc(tr_mm, 1)
            pe.wait_ge(tr_lo, T0 + 2 * q + 2)
            pe.wait_ge(tr_hi, T0 + 2 * q + 2)
            for x in range(4):
                m = 4 * q + x
                pe.wait_ge(sc_add, KT * (NE // 2) + max(m - 1, 0))
                cols = slice(128 * x, 128 * x + 128)
                for hh in range(2):
                    nc.tensor.matmul(pt[:, m % 2, 0:NC], yhi[:, hh, cols], stx[:, hh, :], start=hh == 0, stop=False)
                    last = nc.tensor.matmul(pt[:, m % 2, 0:NC], ylo[:, hh, cols], stx[:, hh, :], start=False,
                                            stop=hh == 1)
                last.then_inc(sc_mm, 1)
        pe.wait_ge(fin_sum, KT)
        mean_over_channels(hfin, ps, HALF, fin_mm)

    RV_LOGITS = 5
    RV_AFF = 5
    RV_MASK = RV_AFF + 2 + 2 * (CAPL // 8) + 2 * (CAPC // 8) + 1
    RV_MK5 = RV_MASK + 1
    RV_END = RV_MK5 + 1 + 1 + 3
    hfin, o_ = at("hfin", [128, N], F32, R0)
    fsq, o_ = at("fsq", [128, 2, N], F32, o_)
    f1, o_ = at("f1", [128, N], F32, o_)
    f2, o_ = at("f2", [128, N], F32, o_)
    f3, o_ = at("f3", [128, N], F32, o_)

    def scalar_program(act):
        def split_hi(slot, use, d, dk):
            act.wait_ge(raw_loaded[slot], 16 * (use + 1))
            act.wait_ge(dense_mm, d_done(d))
            nc.scalar.copy(whi[:, dk, :], raw[:, slot, :]).then_inc(hi_ready, 1)
            act.wait_ge(hi_ready, d + 1)
            act.sem_inc(raw_freed[slot], 1)

        def ada_read_out(slot, use, n, bank):
            act.wait_ge(raw_freed[slot], 2 * use + 2)
            act.wait_ge(small_loaded, 16 * 7)
            nc.scalar.activation(mod[:, ds(n, 1), :].rearrange("p a c -> p (a c)"), bank[:, 0:2], ACT.Identity,
                                 bias=bada[:, ds(n, 1)]).then_inc(ada_read, 1)

        act.sem_inc(ada_read, RAW)
        act.wait_ge(small_loaded, 16 * 7)
        nc.scalar.activation(cond[:, :, :], cond[:, :, :], ACT.Silu).then_inc(cond_ready, 1)
        for kt in range(KT):
            act.wait_ge(x_loaded[kt // 4], 16)
            if kt >= 2:
                act.wait_ge(sq_summed, kt - 1)
            nc.scalar.activation((t2 if kt % 2 else t3)[:, :], xin[:, kt, :], ACT.Square).then_inc(sq_made, 1)
        with act.Fori(0, A1 // RAW) as i:
            for k in range(RAW):
                ada_read_out(*raw_use(0, 1, RAW, i, k), i * RAW + k, pu[:, k, :])
        act.wait_ge(norm_t, 2)
        nc.scalar.activation(rstd[:, :], t2[:, :], ACT.Sqrt).then_inc(norm_sq, 1)
        act.wait_ge(gsc_ready, 1)
        for kt in range(KT):
            act.wait_ge(xn_ready, kt + 1)
            nc.scalar.activation(hhi[:, kt, 0:NL], xin[:, kt, 0:NL], ACT.Identity, scale=gsc[:, kt, 0:1],
                                 bias=mod[:, kt, 0:1])
            nc.scalar.activation(hhi[:, kt, NL:N], xin[:, kt, NL:N], ACT.Identity, scale=gsc[:, kt, 1:2],
                                 bias=mod[:, kt, 1:2]).then_inc(h_hi, 1)

        def ahead(i, k, body, first, stride, d0, count, nxt):
            if isinstance(i, int) and i * body + k + 2 >= count:
                if nxt is None:
                    return None
                m = i * body + k + 2 - count
                return (*raw_use(nxt, 1, U, 0, m), d0 + count + m)
            return (*raw_use(first, stride, body, i, k + 2), i * body + (d0 + k + 2))

        scalar_program.ahead = ahead
        act.wait_ge(h_lo, KT)
        for d in range(2):
            split_hi(*raw_use(G_Q, 1, U, 0, d), d, d % 2)
        for d in range(2 * NKV):
            if d < NKV:
                act.wait_ge(dense_mm, d + 1 + CREDIT)
                if d:
                    act.wait_ge(v_tr, d)
                    act.wait_ge(vx_stored, 16 * d)
                nc.scalar.copy(vst[:, :].rearrange("p (c n) -> p c n", c=2),
                               pu[:, 2 * (d % 2):2 * (d % 2) + 2, 0:HALF]).then_inc(v_read, 1)
                act.wait_ge(v_read, d + 1)
                act.sem_inc(psum_free[d % 2], 1)
            if 1 <= d <= NKV:
                n = d - 1
                act.wait_ge(v_tr, n + 1)
                if n:
                    act.wait_ge(v_stored, 16 * n)
                nc.scalar.copy(vtk[:, 0:640], pt[:, :, :].rearrange("p b n -> p (b n)")[:, 0:640]).then_inc(v_tok, 1)
            split_hi(*raw_use(G_Q, 1, U, 0, d + 2), d + 2, d % 2)
        with act.Fori(2 * NKV // U, QN // U) as i:
            for k in range(U):
                slot, use, d2 = ahead(i, k, U, G_Q, 1, 0, QN, G_G)
                split_hi(slot, use, d2, k % 2)

        def glu(i, k):
            n = i * U + k
            if k % 2 == 0:
                act.wait_ge(dense_mm, n + (QN + 1 + CREDIT))
                act.wait_ge(glu_z, i * (U // 2) + k // 2)
                nc.scalar.activation(gsig[:, :].rearrange("p (c n) -> p c n", c=2),
                                     pu[:, 2 * (k % 2):2 * (k % 2) + 2, 0:HALF], ACT.Sigmoid).then_inc(glu_sig, 1)
                act.wait_ge(glu_sig, i * (U // 2) + k // 2 + 1)
                act.sem_inc(psum_free[0], 1)
            got = ahead(i, k, U, G_G, 1, QN, GN, None)
            if got is None:
                m = i * U + k + 2 - GN
                slot, use = raw_use(G_S, 3, US, 0, m)
                got = (slot, use, QN + GN + m)
            split_hi(*got, k % 2)

        with act.Fori(0, GN // U - 1) as i:
            for k in range(U):
                glu(i, k)
        for k in range(U):
            glu(GN // U - 1, k)

        def softmax(i, n):
            h, j = STEPS[n]
            lo, hi = keys_of(j)
            w = 128 * (hi - lo)
            act.wait_ge(att_nm, i * NS + (n + 1))
            head = ds(i * GROUP + h, 1)
            if j < 4:
                nc.scalar.activation(pe_[:, 0:w], sm[:, 0:w], ACT.Exp, bias=nm[:, 0:1], scale=SCALE,
                                     accum_out=dn[:, 0:1])
                nc.scalar.activation(dn[:, 1:2], sinks[:, head], ACT.Exp, bias=nm[:, 0:1])
                nc.scalar.activation(pe_[:, w:w + PAST], ps[:, 1, 0:PAST], ACT.Exp, bias=nm[:, 0:1], scale=SCALE,
                                     accum_out=dn[:, 2:3]).then_inc(att_exp, 1)
            else:
                nc.scalar.activation(pe_[:, 0:NC], ps[:, 0, 0:NC], ACT.Exp, bias=nm[:, 0:1], scale=SCALE,
                                     accum_out=dn[:, 0:1])
                nc.scalar.activation(dn[:, 1:2], sinks[:, head], ACT.Exp, bias=nm[:, 0:1]).then_inc(att_exp, 1)

        def turned(i, n):
            h, j = STEPS[n]
            lo, hi = keys_of(j)
            w = 128 * (hi - lo + 2) if j < 4 else 128
            act.wait_ge(att_tr, i * NS + (n + 1))
            last = nc.scalar.copy(pt_sb[:, 0:min(w, 512)], pt[:, 0, 0:min(w, 512)])
            if w > 512:
                last = nc.scalar.copy(pt_sb[:, 512:w], ps[:, 1, 0:w - 512])
            last.then_inc(att_pt, 1)

        def head_out(i, n):
            act.wait_ge(att_pv, i * NS + (n + 1))
            if n >= 2:
                act.wait_ge(att_stored[n % 2], (i * (NS // 2) + n // 2) * 16)
            else:
                act.wait_ge(att_stored[n % 2], (i * (NS // 2)) * 16)
            nc.scalar.copy(ao[:, n % 2, :], pt[:, 0, 0:128]).then_inc(att_out, 1)

        def stage_s(i):
            for k in range(US):
                steps = list(range(CUT[k], CUT[k + 1]))
                for x, n in enumerate(steps):
                    softmax(i, n)
                    turned(i, n)
                    if x < 2:
                        at_ = G_S + 3 * k + 1 + x
                        ada_read_out(at_ % RAW, at_ // RAW + i * (3 * US // RAW), i * (2 * US) + (A1 + 2 * k + x),
                                     pt[:, 1, :])
                    head_out(i, n)
                act.wait_ge(dense_mm, i * US + (QN + GN + k + 1 + CREDIT))
                act.wait_ge(th_stored[k % 2], (i * (US // 2) + k // 2) * 16)
                nc.scalar.activation(th[:, k % 2, :].rearrange("p (c n) -> p c n", c=2),
                                     pu[:, 2 * (k % 2):2 * (k % 2) + 2, 0:HALF], ACT.Tanh,
                                     scale=0.5).then_inc(th_ready, 1)
                act.wait_ge(th_ready, i * US + (k + 1))
                act.sem_inc(psum_free[k % 2], 1)
                slot, use, d2 = ahead(i, k, US, G_S, 3, QN + GN, SN, G_T)
                split_hi(slot, use, d2, k % 2)

        with act.Fori(0, SN // US - 1) as i:
            stage_s(i)
        stage_s(SN // US - 1)

        D_T = QN + GN + SN
        act.wait_ge(dense_mm, D_T + CREDIT)
        for m in range(KT):
            act.wait_ge(attn_loaded[m % 4], 16 * (m // 4 + 1))
            nc.scalar.copy(hhi[:, m, :], att4[:, m % 4, :]).then_inc(attn_hi, 1)

        def ln_squares():
            for m in range(CT):
                act.wait_ge(ln_c, 1 + m + 1)
                if m >= 2:
                    act.wait_ge(ln_sum2, m - 1)
                nc.scalar.activation(lq[:, m % 2, 0:CO], zt[:, m, 0:CO], ACT.Square).then_inc(ln_sq, 1)

        def ln_root():
            act.wait_ge(ln_c, LN_R)
            nc.scalar.activation(ls2[:, 0:CO], ls3[:, 0:CO], ACT.Sqrt).then_inc(norm_sq, 1)

        def ln_swish():
            act.wait_ge(ln_c, LN_RSTD)
            for m in range(CT):
                act.wait_ge(ln_c, LN_RSTD + m + 1)
                if m >= 2:
                    act.wait_ge(ln_lo, m - 1)
                row = lt2 if m % 2 else lt1
                for c0, z0, w in ((0, 0, NL), (NL, NL + 2 * PAD, NC)):
                    last = nc.scalar.activation(row[:, c0:c0 + w], zt[:, m, z0:z0 + w], ACT.Silu,
                                                scale=convp[:, 1, m:m + 1], bias=convp[:, 2, m:m + 1])
                last.then_inc(ln_act, 1)
                act.wait_ge(ln_act, m + 1)
                if m == 0:
                    act.wait_ge(ln_c, LN_RSTD + CT)
                nc.scalar.copy(ahi[:, m, :], row[:, 0:N]).then_inc(ln_hi, 1)

        def finish_split(t, base_d, first, n_next, n):
            if t + 2 < n:
                split_hi(*raw_use(first, 1, U, 0, t + 2), base_d + t + 2, t % 2)
            elif n_next is not None:
                split_hi(*raw_use(n_next, 1, U, 0, t + 2 - n), base_d + t + 2, t % 2)

        for t in range(TN):
            act.wait_ge(dense_mm, D_T + t + 1 + CREDIT)
            finish_split(t, D_T, G_T, G_C, TN)
            if t == 1:
                ln_squares()
            if t == 3:
                ln_root()
            if t == 4:
                ln_swish()
        for m in range(KT):
            act.wait_ge(mix_sum, m + 1)
            nc.scalar.copy(hhi[:, m, :], (lt2 if m % 2 else lt1)[:, 0:N]).then_inc(mix_hi, 1)
            if m % 2:
                c = m // 2
                finish_split(c, D_T + TN, G_C, G_O, CN)
        for t in range(ON):
            act.wait_ge(res_done, t + 1)
            if t:
                act.wait_ge(res_sum, t)
            nc.scalar.activation(sq[:, :], xr[:, t, :], ACT.Square).then_inc(res_sq, 1)
            finish_split(t, D_T + TN + CN, G_O, None, ON)
        act.wait_ge(norm_t, 4 + 4)
        nc.scalar.activation(e1[:, :], e3[:, :], ACT.Sqrt).then_inc(norm_sq, 1)
        for kt in range(KT):
            act.wait_ge(h2_vec, kt + 1)
            if kt:
                act.wait_ge(h2_tr, kt)
            row = (e2 if kt % 2 else e3)
            nc.scalar.activation(h2t[:, 0, 0:NL], row[:, 0:NL], ACT.Identity, scale=gsc[:, kt, 0:1],
                                 bias=mod[:, 3 * KT + kt, 0:1])
            nc.scalar.activation(h2t[:, 0, NL:N], row[:, NL:N], ACT.Identity, scale=gsc[:, kt, 1:2],
                                 bias=mod[:, 3 * KT + kt, 1:2]).then_inc(h2_act, 1)
            if kt >= 1:
                turned_hi(kt - 1)
        turned_hi(KT - 1)
        act.wait_ge(h2_tr, KT)
        nc.scalar.activation(lgT[:, :], ps[0:16, :, :].rearrange("p b n -> p (b n)")[:, 0:N], ACT.Identity,
                             bias=brt[:, 0:1]).then_inc(rt_act, 1)
        act.wait_ge(rt_vec, 2)
        nc.scalar.activation(sm5[:, :, :], sm5[:, :, :], ACT.Exp).then_inc(rt_act, 1)

        def silus(e, n):
            for b in range(4):
                slot, use = raw_use(G_E, 1, 3 * FT, e, 4 * b + 3)
                act.wait_ge(raw_freed[slot], 2 * use + 2)
                act.wait_ge(gu_hid, n * 4 + b)
                v = pu[:, b % 2, 0:4 * CAP].rearrange("p (m g s) -> p m g s", m=2, g=2)
                nc.scalar.activation(sil[:, :, :], v[:, :, 0, :], ACT.Silu).then_inc(gu_sil, 1)

        def downs(e, n, half, ctx_at):
            for m in range(FT):
                slot, use = raw_use(G_E, 1, 3 * FT, e, 2 * FT + m)
                act.wait_ge(raw_freed[slot], 2 * use + 2)
                v = pu[:, 2 + m % 2, 0:2 * CAP].rearrange("p (b s) -> p b s", b=2)
                nc.scalar.copy(yt[:, 2 * m:2 * m + 2, 64 * half:64 * half + 64], v[:, :, 0:CAPL])
                nc.scalar.copy(ytc[:, 2 * m:2 * m + 2, ds(ctx_at, 16)], v[:, :, CAPL:CAP]).then_inc(dn_read, 1)

        act.wait_ge(rt_vec, RV_END)
        for b in range(KT // 4):
            act.wait_ge(ga_mm, b + 1)
            nc.scalar.copy(xe[:, 4 * b:4 * b + 4, :],
                           ps[:, b % 2, 0:4 * CAP].rearrange("p (k s) -> p k s", s=CAP)).then_inc(ga_read, 1)
        with act.Fori(0, NE // 2) as pair:
            act.wait_ge(sel_st, pair + 1)
            act.wait_ge(sc_mm, pair * KT)
            nc.scalar.copy(gates[:, 0:1], pt[:, 1, 0:1])
            nc.scalar.copy(stt_[:, :], pt[:, 0, :]).then_inc(st_read, 1)
            for half in range(2):
                e = pair * 2 + half
                silus(e, e)
                for b in range(KT // 4):
                    act.wait_ge(ga_mm, e * 4 + (4 + b + 1))
                    nc.scalar.copy(xe[:, 4 * b:4 * b + 4, :],
                                   ps[:, b % 2, 0:4 * CAP].rearrange("p (k s) -> p k s", s=CAP)).then_inc(ga_read, 1)
                downs(e, e, half, e * CAPC)
            for q in range(KT // 4):
                act.wait_ge(tr_mm, pair * 4 + (q + 1))
                if q >= 2:
                    act.wait_ge(sc_mm, pair * KT + 4 * (q - 1))
                nc.scalar.activation(yhi[:, q % 2, :], ps[:, q % 2, :], ACT.Identity,
                                     scale=gates[:, 0:1]).then_inc(tr_hi, 1)
        act.wait_ge(sel_st, NE // 2 + 1)
        act.wait_ge(sc_mm, KT * (NE // 2))
        nc.scalar.copy(gates[:, 2:4], pt[:, 1, 0:2])
        nc.scalar.copy(stx[:, :, :], pt[:, 0, 0:256].rearrange("p (h n) -> p h n", h=2)).then_inc(st_read, 1)
        act.wait_ge(st_read, NE // 2 + 1)
        for q in range(KT // 4):
            for hh in range(2):
                n = 4 * (NE // 2) + 2 * q + hh
                act.wait_ge(tr_mm, n + 1)
                act.wait_ge(sc_mm, KT * (NE // 2) + 4 * q)
                nc.scalar.activation(yhi[:, hh, :], ps[:, hh, :], ACT.Identity,
                                     scale=gates[:, 2 + hh:3 + hh]).then_inc(tr_hi, 1)
        for kt in range(KT):
            act.wait_ge(sc_add, KT * (NE // 2) + kt + 1)
            if kt >= 2:
                act.wait_ge(fin_sum, kt - 1)
            nc.scalar.activation(fsq[:, kt % 2, :], xr[:, kt, :], ACT.Square).then_inc(fin_sq, 1)
        act.wait_ge(fin_c, 2)
        nc.scalar.activation(f1[:, :], f3[:, :], ACT.Sqrt).then_inc(norm_sq, 1)

    def d_done(d):
        D_C = QN + GN + SN + TN
        if isinstance(d, int):
            prev = d - SPL
            if prev < D_C:
                return prev + 1 + CREDIT
            if prev < D_C + CN:
                return D_C + 2 * (prev - D_C + 1) + CREDIT
            return prev + CN + 1 + CREDIT
        return d + (1 + CREDIT - SPL)

    LN_R = 1 + CT + 2
    LN_RSTD = LN_R + 4
    ln_sum2 = sem("ln_sum2")

    def turned_hi(kt):
        nc.scalar.wait_ge(h2_tr, kt + 1)
        nc.scalar.copy(h2hi[:, :, kt * 128:kt * 128 + 128],
                       pu[:, 2 * (kt % 2):2 * (kt % 2) + 2, :].rearrange("p b n -> p (b n)")[:, 0:640]
                       .rearrange("p (t c) -> p t c", c=128)).then_inc(h2_hi, 1)

    def vector_program(vec):
        chain = [0]

        def link(ins):
            chain[0] += 1
            ins.then_inc(vec_done, 1)
            vec.wait_ge(vec_done, chain[0])

        def split_lo(slot, use, d, dk):
            vec.wait_ge(hi_ready, d + 1)
            nc.vector.tensor_tensor(wlo[:, dk, :], raw[:, slot, :], whi[:, dk, :].bitcast(F32),
                                    ALU.subtract).then_inc(lo_ready, 1)
            vec.wait_ge(lo_ready, d + 1)
            vec.sem_inc(raw_freed[slot], 1)

        ahead = scalar_program.ahead
        for b in range(2):
            vec.sem_inc(psum_free[b], 1)
        nc.vector.memset(t1[:, :], 0.0).then_inc(norm_t, 1)
        for kt in range(KT):
            vec.wait_ge(sq_made, kt + 1)
            if kt == 0:
                vec.wait_ge(norm_t, 1)
            else:
                vec.wait_ge(sq_summed, kt)
            nc.vector.tensor_tensor(t1[:, :], t1[:, :], (t2 if kt % 2 else t3)[:, :], ALU.add).then_inc(sq_summed, 1)
        vec.wait_ge(norm_mm, 1)
        c2 = "p (c n) -> p c n"
        link(nc.vector.tensor_scalar(t4[:, :].rearrange(c2, c=2), pu[:, 0:2, 0:HALF], EPS, None, ALU.add))
        nc.vector.reciprocal(t2[:, :], t4[:, :]).then_inc(norm_t, 1)
        vec.wait_ge(norm_sq, 1)
        link(nc.vector.tensor_tensor(t3[:, :], rstd[:, :], rstd[:, :], ALU.mult))
        link(nc.vector.tensor_tensor(t3[:, :], t3[:, :], t4[:, :], ALU.mult))
        link(nc.vector.tensor_scalar(t3[:, :], t3[:, :], -0.5, 1.5, ALU.mult, ALU.add))
        link(nc.vector.tensor_tensor(rstd[:, :], rstd[:, :], t3[:, :], ALU.mult))
        vec.wait_ge(ada_read, RAW + A1)
        vec.wait_ge(small_loaded, 16 * 7)
        nc.vector.tensor_scalar(negsink[:, :], sinks[:, :], -1.0, None, ALU.mult)
        nc.vector.scalar_tensor_tensor(out=gsc[:, :, :], in0=mod[:, KT:2 * KT, :], scalar=1.0,
                                       in1=norms[:, 0, :, :], op0=ALU.add, op1=ALU.mult).then_inc(gsc_ready, 1)
        for kt in range(KT):
            nc.vector.tensor_tensor(xin[:, kt, :], xin[:, kt, :], rstd[:, :], ALU.mult).then_inc(xn_ready, 1)
        vec.wait_ge(gsc_ready, 1)
        for kt in range(KT):
            vec.wait_ge(h_hi, kt + 1)
            vec.wait_ge(xn_ready, kt + 1)
            nc.vector.tensor_scalar(xin[:, kt, 0:NL], xin[:, kt, 0:NL], gsc[:, kt, 0:1], mod[:, kt, 0:1],
                                    ALU.mult, ALU.add)
            link(nc.vector.tensor_scalar(xin[:, kt, NL:N], xin[:, kt, NL:N], gsc[:, kt, 1:2], mod[:, kt, 1:2],
                                         ALU.mult, ALU.add))
            nc.vector.tensor_tensor(hlo[:, kt, :], xin[:, kt, :], hhi[:, kt, :].bitcast(F32),
                                    ALU.subtract).then_inc(h_lo, 1)
        for d in range(2):
            split_lo(*raw_use(G_Q, 1, U, 0, d), d, d % 2)

        def rotate(i, d, k, n):
            vec.wait_ge(dense_mm, d + (1 + CREDIT))
            src = pu[:, 2 * (k % 2):2 * (k % 2) + 2, 0:HALF]
            vec.wait_ge(rope_out, n)
            nc.vector.tensor_tensor(ra[:, :].rearrange(c2, c=2), src, cost[:, :].rearrange(c2, c=2),
                                    ALU.mult).then_inc(rope_a, 1)
            nc.vector.tensor_tensor(rb[:, :].rearrange(c2, c=2), src, sint[:, :].rearrange(c2, c=2),
                                    ALU.mult).then_inc(rope_b, 1)
            vec.wait_ge(rope_b, n + 1)
            vec.sem_inc(psum_free[k % 2], 1)
            vec.wait_ge(rope_swapped, n * 64 + 64)
            if i is None:
                stored = 32 * n
            else:
                stored = n * 16 + 16 * NKV
            vec.wait_ge(rope_stored, stored)
            nc.vector.tensor_tensor(ro[:, :], ra[:, :], rbs[:, :], ALU.add).then_inc(rope_out, 1)

        for d in range(2 * NKV):
            if d >= NKV:
                if d == NKV:
                    vec.wait_ge(tabs_loaded, 48)
                rotate(None, d, d % 2, d - NKV)
            split_lo(*raw_use(G_Q, 1, U, 0, d + 2), d + 2, d % 2)
        with vec.Fori(2 * NKV // U, QN // U) as i:
            for k in range(U):
                rotate(i, i * U + k, k, i * U + (k - NKV))
                slot, use, d2 = ahead(i, k, U, G_Q, 1, 0, QN, G_G)
                split_lo(slot, use, d2, k % 2)
        vec.wait_ge(rope_stored, 16 * (2 * NKV + NH))
        vec.wait_ge(v_stored, 16 * NKV)
        vec.wait_ge(vx_stored, 16 * NKV)
        nc.vector.memset(zt[:, :, 0:PAD], 0.0)
        nc.vector.memset(zt[:, :, PAD + NL:PAD + NL + 2 * PAD], 0.0)
        nc.vector.memset(zt[:, :, ZW - PAD:ZW], 0.0).then_inc(z_zero, 1)
        ztf = zt[:, :, :].rearrange("p m c -> p (m c)")

        def glu(i, k):
            if k % 2 == 1:
                vec.wait_ge(dense_mm, i * U + (QN + k + 1 + CREDIT))
                vec.wait_ge(glu_sig, i * (U // 2) + (k // 2 + 1))
                for t, c, c0, c1 in SEGS:
                    z0 = i * (U // 2 * ZW) + (k // 2 * ZW + PAD + t + (2 * PAD if t >= NL else 0))
                    last = nc.vector.tensor_tensor(ztf[:, ds(z0, c1 - c0)], pu[:, 2 + c, c0:c1],
                                                   gsig[:, t:t + c1 - c0], ALU.mult)
                last.then_inc(glu_z, 1)
                vec.wait_ge(glu_z, i * (U // 2) + (k // 2 + 1))
                vec.sem_inc(psum_free[1], 1)
            got = ahead(i, k, U, G_G, 1, QN, GN, None)
            if got is None:
                m = i * U + k + 2 - GN
                got = (*raw_use(G_S, 3, US, 0, m), QN + GN + m)
            split_lo(*got, k % 2)

        with vec.Fori(0, GN // U - 1) as i:
            for k in range(U):
                glu(i, k)
        for k in range(U):
            glu(GN // U - 1, k)

        def maxima(i, n):
            h, j = STEPS[n]
            lo, hi = keys_of(j)
            w = 128 * (hi - lo)
            s = i * NS + n
            vec.wait_ge(att_qk, s + 11)
            v = i * (4 * NS) + 4 * n
            if j < 4:
                nc.vector.reduce_max(mx[:, 0:1], ps[:, 1, 0:PAST], AX).then_inc(att_v, 1)
                vec.wait_ge(att_v, v + 1)
                vec.sem_inc(vec_passed, 1)
                m0 = 128 if j == 0 else 0
                nc.vector.tensor_tensor_reduce(out=sm[:, 0:w], in0=ps[:, 0, 0:w], in1=mask[:, m0:m0 + w], scale=1.0,
                                               scalar=mx[:, 0:1], op0=ALU.add, op1=ALU.max,
                                               accum_out=mx[:, 1:2]).then_inc(att_v, 1)
            else:
                nc.vector.reduce_max(mx[:, 1:2], ps[:, 0, 0:NC], AX).then_inc(att_v, 2)
            vec.wait_ge(att_v, v + 2)
            nc.vector.tensor_scalar(nm[:, 0:1], mx[:, 1:2], -SCALE, negsink[:, ds(i * GROUP + h, 1)], ALU.mult,
                                    ALU.min).then_inc(att_nm, 1)

        def normalise(i, n):
            h, j = STEPS[n]
            lo, hi = keys_of(j)
            w = 128 * (hi - lo) + PAST if j < 4 else NC
            v = i * (4 * NS) + 4 * n
            vec.wait_ge(att_exp, i * NS + (n + 1))
            nc.vector.reduce_sum(rd[:, 0:1], dn[:, 0:3 if j < 4 else 2], AX).then_inc(att_v, 1)
            vec.wait_ge(att_v, v + 3)
            nc.vector.reciprocal(rd[:, 1:2], rd[:, 0:1]).then_inc(att_v, 1)
            vec.wait_ge(att_v, v + 4)
            vec.wait_ge(att_tr, i * NS + n)
            nc.vector.tensor_scalar(pn[:, 0:w], pe_[:, 0:w], rd[:, 1:2], None, ALU.mult).then_inc(att_pn, 1)

        def conv(i, k, part, parts):
            m_off = k // 4
            lo_ = (k % 4) * 8
            taps_ = list(range(lo_, min(lo_ + 8, TAPS)))
            a0, a1 = len(taps_) * part // parts, len(taps_) * (part + 1) // parts
            for x in taps_[a0:a1]:
                tap = TAPS - 1 - x
                done = i * (2 * TAPS) + (m_off * TAPS + x)
                zb = i * (2 * ZW) + (m_off * ZW + tap)
                w = taps[:, :, :].rearrange("p m t -> p (m t)")[:, ds(i * (2 * TAPS) + (m_off * TAPS + tap), 1)]
                vec.wait_ge(conv_done, done)
                if x == 0:
                    nc.vector.tensor_scalar(ctmp[:, :], ztf[:, ds(zb, CO)], w, convp[:, 0, ds(i * 2 + m_off, 1)],
                                            ALU.mult, ALU.add).then_inc(conv_done, 1)
                else:
                    dst = ctmp[:, :] if tap else ztf[:, ds(zb, CO)]
                    nc.vector.scalar_tensor_tensor(out=dst, in0=ztf[:, ds(zb, CO)], scalar=w, in1=ctmp[:, :],
                                                   op0=ALU.mult, op1=ALU.add).then_inc(conv_done, 1)

        vec.wait_ge(z_zero, 1)
        vec.wait_ge(tabs_loaded, 48)

        def stage_s(i):
            for k in range(US):
                steps = list(range(CUT[k], CUT[k + 1]))
                for x, n in enumerate(steps):
                    maxima(i, n)
                    normalise(i, n)
                    conv(i, k, x, len(steps))
                vec.wait_ge(dense_mm, i * US + (QN + GN + k + 1 + CREDIT))
                slot, use, d2 = ahead(i, k, US, G_S, 3, QN + GN, SN, G_T)
                split_lo(slot, use, d2, k % 2)

        with vec.Fori(0, SN // US - 1) as i:
            stage_s(i)
        stage_s(SN // US - 1)

        D_T = QN + GN + SN
        vec.wait_ge(ada_read, RAW + ADA)
        nc.vector.tensor_scalar(ghalf[:, :, :], mod[:, 2 * KT:3 * KT, :], 0.5, None, ALU.mult)
        link(nc.vector.scalar_tensor_tensor(out=gsc[:, :, :], in0=mod[:, 4 * KT:5 * KT, :], scalar=1.0,
                                            in1=norms[:, 1, :, :], op0=ALU.add, op1=ALU.mult))
        for m in range(KT):
            vec.wait_ge(attn_hi, m + 1)
            nc.vector.tensor_tensor(hlo[:, m, :], att4[:, m % 4, :], hhi[:, m, :].bitcast(F32),
                                    ALU.subtract).then_inc(attn_lo, 1)

        def finish_split(t, base_d, first, n_next, n):
            if t + 2 < n:
                split_lo(*raw_use(first, 1, U, 0, t + 2), base_d + t + 2, t % 2)
            elif n_next is not None:
                split_lo(*raw_use(n_next, 1, U, 0, t + 2 - n), base_d + t + 2, t % 2)

        lnc = [0]

        def ln(ins):
            lnc[0] += 1
            ins.then_inc(ln_c, 1)

        def ln_link(ins):
            ln(ins)
            vec.wait_ge(ln_c, lnc[0])

        def ln_mean():
            vec.wait_ge(conv_done, TAPS * CT)
            nc.vector.tensor_reduce(ls1[:, 0:CO], zt[:, :, 0:CO].rearrange("p m c -> p c m"), AX,
                                    ALU.add).then_inc(ln_sum, 1)

        def ln_centre():
            vec.wait_ge(ln_mm, 1)
            ln_link(nc.vector.tensor_scalar(ls2[:, 0:CO].rearrange(c2, c=2), ps[:, :, 0:CO // 2], D / CW, None,
                                            ALU.mult))
            for m in range(CT):
                ln(nc.vector.tensor_tensor(zt[:, m, 0:CO], zt[:, m, 0:CO], ls2[:, 0:CO], ALU.subtract))
            for m in range(CT):
                vec.wait_ge(ln_sq, m + 1)
                row = lq[:, m % 2, 0:CO]
                if m == 0:
                    nc.vector.tensor_copy(ls1[:, 0:CO], row).then_inc(ln_sum2, 1)
                else:
                    vec.wait_ge(ln_sum2, m)
                    nc.vector.tensor_tensor(ls1[:, 0:CO], ls1[:, 0:CO], row, ALU.add).then_inc(
                        ln_sum2 if m < CT - 1 else ln_sum, 1)

        def ln_rstd():
            vec.wait_ge(ln_mm, 2)
            ln_link(nc.vector.tensor_scalar(ls1[:, 0:CO].rearrange(c2, c=2), pt[:, :, 0:CO // 2], D / CW, EPS,
                                            ALU.mult, ALU.add))
            ln_link(nc.vector.reciprocal(ls3[:, 0:CO], ls1[:, 0:CO]))
            assert lnc[0] == LN_R, lnc
            vec.wait_ge(norm_sq, 2)
            ln_link(nc.vector.tensor_tensor(ls3[:, 0:CO], ls2[:, 0:CO], ls2[:, 0:CO], ALU.mult))
            ln_link(nc.vector.tensor_tensor(ls3[:, 0:CO], ls3[:, 0:CO], ls1[:, 0:CO], ALU.mult))
            ln_link(nc.vector.tensor_scalar(ls3[:, 0:CO], ls3[:, 0:CO], -0.5, 1.5, ALU.mult, ALU.add))
            ln_link(nc.vector.tensor_tensor(ls2[:, 0:CO], ls2[:, 0:CO], ls3[:, 0:CO], ALU.mult))
            assert lnc[0] == LN_RSTD, lnc
            for m in range(CT):
                ln(nc.vector.tensor_tensor(zt[:, m, 0:CO], zt[:, m, 0:CO], ls2[:, 0:CO], ALU.mult))

        def ln_low():
            for m in range(CT):
                vec.wait_ge(ln_hi, m + 1)
                row = lt2 if m % 2 else lt1
                nc.vector.tensor_tensor(alo[:, m, :], row[:, 0:N], ahi[:, m, :].bitcast(F32),
                                        ALU.subtract).then_inc(ln_lo, 1)

        vec.wait_ge(attn_lo, KT)
        for t in range(TN):
            vec.wait_ge(dense_mm, D_T + t + 1 + CREDIT)
            vec.wait_ge(gl_loaded[t % 2], 16 * (t // 2 + 1))
            if t >= 2:
                vec.wait_ge(mo_stored[t % 2], 16 * (t // 2))
            nc.vector.scalar_tensor_tensor(out=mo[:, t % 2, :].rearrange(c2, c=2),
                                           in0=gl[:, t % 2, :].rearrange(c2, c=2), scalar=1.0,
                                           in1=pu[:, 2 * (t % 2):2 * (t % 2) + 2, 0:HALF], op0=ALU.add,
                                           op1=ALU.mult).then_inc(mo_ready, 1)
            vec.wait_ge(mo_ready, t + 1)
            vec.sem_inc(psum_free[t % 2], 1)
            finish_split(t, D_T, G_T, G_C, TN)
            if t == 0:
                ln_mean()
            if t == 1:
                ln_centre()
            if t == 3:
                ln_rstd()
            if t == 4:
                ln_low()
        for m in range(KT):
            p = D_T + TN + m
            vec.wait_ge(dense_mm, p + 1 + CREDIT)
            use = KT // 2 + m // 2 + 1
            vec.wait_ge(gl_loaded[m % 2], 16 * use)
            vec.wait_ge(ml_loaded[m % 2], 16 * (m // 2 + 1))
            row = (lt2 if m % 2 else lt1)[:, 0:N]
            if m >= 2:
                vec.wait_ge(mix_hi, m - 1)
            link(nc.vector.scalar_tensor_tensor(out=row.rearrange(c2, c=2), in0=gl[:, m % 2, :].rearrange(c2, c=2),
                                                scalar=1.0, in1=pu[:, 2 * (m % 2):2 * (m % 2) + 2, 0:HALF],
                                                op0=ALU.add, op1=ALU.mult))
            vec.sem_inc(psum_free[m % 2], 1)
            nc.vector.tensor_tensor(row, row, mo[:, m % 2, :], ALU.add).then_inc(mix_sum, 1)
            vec.wait_ge(mix_hi, m + 1)
            nc.vector.tensor_tensor(hlo[:, m, :], row, hhi[:, m, :].bitcast(F32), ALU.subtract).then_inc(mix_lo, 1)
            if m % 2:
                finish_split(m // 2, D_T + TN, G_C, G_O, CN)
        link(nc.vector.memset(ssum[:, :], 0.0))
        vec.wait_ge(xr_loaded, 64)
        for t in range(ON):
            p = D_T + TN + 2 * CN + t
            vec.wait_ge(dense_mm, p + 1 + CREDIT)
            for t0, c, c0, c1 in SEGS:
                s = 1 if t0 >= NL else 0
                last = nc.vector.scalar_tensor_tensor(out=xr[:, t, t0:t0 + c1 - c0],
                                                      in0=pu[:, 2 * (t % 2) + c, c0:c1],
                                                      scalar=ghalf[:, t, s:s + 1], in1=xr[:, t, t0:t0 + c1 - c0],
                                                      op0=ALU.mult, op1=ALU.add)
            last.then_inc(res_done, 1)
            vec.wait_ge(res_done, t + 1)
            vec.sem_inc(psum_free[t % 2], 1)
            finish_split(t, D_T + TN + CN, G_O, None, ON)
            vec.wait_ge(res_sq, t + 1)
            if t:
                vec.wait_ge(res_sum, t)
            nc.vector.tensor_tensor(ssum[:, :], ssum[:, :], sq[:, :], ALU.add).then_inc(res_sum, 1)
        nt = [2]

        def ntl(ins):
            nt[0] += 1
            ins.then_inc(norm_t, 1)
            vec.wait_ge(norm_t, nt[0])

        vec.wait_ge(norm_mm, 2)
        ntl(nc.vector.memset(posm[:, :, :], 0.0))
        ntl(nc.vector.memset(aff[:, :, :], 0.0))
        ntl(nc.vector.memset(top8[:, :], 0.0))
        ntl(nc.vector.memset(mk5[:, :, :], 0.0))
        ntl(nc.vector.tensor_scalar(e2[:, :].rearrange(c2, c=2), ps[:, :, 0:HALF], EPS, None, ALU.add))
        ntl(nc.vector.reciprocal(e3[:, :], e2[:, :]))
        vec.wait_ge(norm_sq, 3)
        ntl(nc.vector.tensor_tensor(e3[:, :], e1[:, :], e1[:, :], ALU.mult))
        ntl(nc.vector.tensor_tensor(e3[:, :], e3[:, :], e2[:, :], ALU.mult))
        ntl(nc.vector.tensor_scalar(e3[:, :], e3[:, :], -0.5, 1.5, ALU.mult, ALU.add))
        ntl(nc.vector.tensor_tensor(e1[:, :], e1[:, :], e3[:, :], ALU.mult))

        def turned_lo(kt):
            vec.wait_ge(h2_hi, kt + 1)
            nc.vector.tensor_tensor(h2lo[:, :, kt * 128:kt * 128 + 128],
                                    pu[:, 2 * (kt % 2):2 * (kt % 2) + 2, :].rearrange("p b n -> p (b n)")[:, 0:640]
                                    .rearrange("p (t c) -> p t c", c=128),
                                    h2hi[:, :, kt * 128:kt * 128 + 128].bitcast(F32), ALU.subtract).then_inc(h2_lo, 1)

        for kt in range(KT):
            if kt >= 2:
                vec.wait_ge(h2_act, kt - 1)
            nc.vector.tensor_tensor((e2 if kt % 2 else e3)[:, :], xr[:, kt, :], e1[:, :], ALU.mult).then_inc(h2_vec, 1)
            if kt >= 2:
                turned_lo(kt - 2)
        turned_lo(KT - 2)
        turned_lo(KT - 1)

        rv = [0]

        def rt(ins):
            rv[0] += 1
            ins.then_inc(rt_vec, 1)
            vec.wait_ge(rt_vec, rv[0])

        vec.wait_ge(rt_pe, 1)
        lg = pt[:, 0, 0:5 * NE].rearrange("p (t e) -> p t e", e=NE)
        rt(nc.vector.tensor_reduce(sm5b[:, :], lg, AX, ALU.max))
        rt(nc.vector.tensor_tensor(sm5[:, :, :], lg, sm5b[:, :].unsqueeze(2).to_broadcast([128, 5, NE]),
                                   ALU.subtract))
        vec.wait_ge(rt_act, 2)
        rt(nc.vector.tensor_reduce(sm5b[:, :], sm5[:, :, :], AX, ALU.add))
        rt(nc.vector.reciprocal(sm5b[:, :], sm5b[:, :]))
        rt(nc.vector.tensor_tensor(aff[:, :, 0:NE], sm5[:, :, :], sm5b[:, :].unsqueeze(2).to_broadcast([128, 5, NE]),
                                   ALU.mult))
        assert rv[0] == RV_AFF
        vec.wait_ge(rt_pe, 2)
        rt(nc.vector.tensor_copy(affT[:, :], ps[0:16, :, :].rearrange("p b n -> p (b n)")[:, 0:N]))
        rt(nc.vector.tensor_copy(work[:, :], affT[:, :]))
        for t0, t1_, cap in ((0, NL, CAPL), (NL, N, CAPC)):
            for r in range(cap // 8):
                rt(nc.vector.max(top8[:, :], work[:, t0:t1_]))
                rt(nc.vector.match_replace(work[:, t0:t1_], top8[:, :], work[:, t0:t1_], -1.0))
        rt(nc.vector.tensor_scalar(work[:, :], work[:, :], 0.0, None, ALU.is_lt))
        assert rv[0] == RV_MASK, (rv, RV_MASK)
        vec.wait_ge(rt_pe, 3)
        rt(nc.vector.tensor_copy(mk5[:, :, :], pt[:, 0, 0:5 * NE].rearrange("p (t e) -> p t e", e=NE)))
        assert rv[0] == RV_MK5
        vec.wait_ge(rt_pe, 4)
        rt(nc.vector.tensor_tensor(posm[:, :, 0:NE], pt[:, 1, 0:5 * NE].rearrange("p (t e) -> p t e", e=NE),
                                   mk5[:, :, :], ALU.mult))
        vec.wait_ge(rt_loaded, 48)
        b3 = [128, NE, CAPC]
        rt(nc.vector.tensor_tensor(scx[:, :].rearrange("p (e s) -> p e s", s=CAPC),
                                   posm[:, 4, 0:NE].unsqueeze(2).to_broadcast(b3),
                                   iota[:, 0:CAPC].unsqueeze(1).to_broadcast(b3), ALU.is_equal))
        rt(nc.vector.tensor_tensor(sgx[:, :].rearrange("p (e s) -> p e s", s=CAPC),
                                   scx[:, :].bitcast(F32).rearrange("p (e s) -> p e s", s=CAPC),
                                   aff[:, 4, 0:NE].unsqueeze(2).to_broadcast(b3), ALU.mult))
        rt(nc.vector.tensor_scalar(sgx[:, :], sgx[:, :], float(D), None, ALU.mult))
        rt(nc.vector.tensor_scalar(aff[:, :, :], aff[:, :, :], float(D), None, ALU.mult))
        assert rv[0] == RV_END, (rv, RV_END)

        selc = sem("sel_chain")

        def select(pair, n):
            b4 = [128, 4, 64]
            for half in range(2):
                e = pair * 2 + half
                col = posm[:, 0:4, ds(e, 1)] if not isinstance(e, int) else posm[:, 0:4, e:e + 1]
                dst = sl[:, :, 64 * half:64 * half + 64]
                nc.vector.tensor_tensor(dst, col.to_broadcast(b4), iota[:, 0:64].unsqueeze(1).to_broadcast(b4),
                                        ALU.is_equal)
                c1 = posm[:, 4, ds(e, 1)] if not isinstance(e, int) else posm[:, 4, e:e + 1]
                last = nc.vector.tensor_tensor(sc[:, 16 * half:16 * half + 16], c1.to_broadcast([128, 16]),
                                               iota[:, 0:16], ALU.is_equal)
            last.then_inc(selc, 1)

        def weigh(pair, n):
            b4 = [128, 4, 64]
            vec.wait_ge(selc, n + 1)
            for half in range(2):
                e = pair * 2 + half
                w = aff[:, 0:4, ds(e, 1)] if not isinstance(e, int) else aff[:, 0:4, e:e + 1]
                last = nc.vector.tensor_tensor(sg[:, :, 64 * half:64 * half + 64],
                                               sl[:, :, 64 * half:64 * half + 64].bitcast(F32), w.to_broadcast(b4),
                                               ALU.mult)
            last.then_inc(sel_made, 1)

        select(0, 0)
        weigh(0, 0)
        with vec.Fori(0, NE // 2) as pair:
            for half in range(2):
                e = pair * 2 + half
                for b in range(4):
                    vec.wait_ge(gu_sil, e * 4 + (b + 1))
                    v = pu[:, b % 2, 0:4 * CAP].rearrange("p (m g s) -> p m g s", m=2, g=2)
                    nc.vector.tensor_tensor(hid[:, 2 * b:2 * b + 2, :], v[:, :, 1, :], sil[:, :, :],
                                            ALU.mult).then_inc(gu_hid, 1)
                if half == 0:
                    vec.wait_ge(ga_mm, pair * 8 + 8)
                    vec.wait_ge(sel_st, pair + 1)
                    select(pair + 1, pair + 1)
                    weigh(pair + 1, pair + 1)
            for q in range(KT // 4 + 1):
                if q < KT // 4:
                    vec.wait_ge(tr_hi, pair * 4 + (q + 1))
                    if q >= 2:
                        vec.wait_ge(sc_mm, pair * KT + 4 * (q - 1))
                    nc.vector.scalar_tensor_tensor(out=ylo[:, q % 2, :], in0=ps[:, q % 2, :], scalar=gates[:, 0:1],
                                                   in1=yhi[:, q % 2, :].bitcast(F32), op0=ALU.mult,
                                                   op1=ALU.subtract).then_inc(tr_lo, 1)
                if q >= 1:
                    for x in range(4):
                        m = 4 * (q - 1) + x
                        vec.wait_ge(sc_mm, pair * KT + (m + 1))
                        nc.vector.scalar_tensor_tensor(out=xr[:, m, 0:NL], in0=pt[:, m % 2, :],
                                                       scalar=mod[:, 5 * KT + m, 0:1], in1=xr[:, m, 0:NL],
                                                       op0=ALU.mult, op1=ALU.add).then_inc(sc_add, 1)
        for q in range(KT // 4):
            for hh in range(2):
                n = 4 * (NE // 2) + 2 * q + hh
                vec.wait_ge(tr_hi, n + 1)
                nc.vector.scalar_tensor_tensor(out=ylo[:, hh, :], in0=ps[:, hh, :], scalar=gates[:, 2 + hh:3 + hh],
                                               in1=yhi[:, hh, :].bitcast(F32), op0=ALU.mult,
                                               op1=ALU.subtract).then_inc(tr_lo, 1)
            for x in range(4):
                m = 4 * q + x
                vec.wait_ge(sc_mm, KT * (NE // 2) + m + 1)
                nc.vector.scalar_tensor_tensor(out=xr[:, m, NL:N], in0=pt[:, m % 2, 0:NC],
                                               scalar=mod[:, 5 * KT + m, 1:2], in1=xr[:, m, NL:N],
                                               op0=ALU.mult, op1=ALU.add).then_inc(sc_add, 1)
        for kt in range(KT):
            vec.wait_ge(fin_sq, kt + 1)
            if kt == 0:
                nc.vector.tensor_copy(hfin[:, :], fsq[:, 0, :]).then_inc(fin_sum, 1)
            else:
                vec.wait_ge(fin_sum, kt)
                nc.vector.tensor_tensor(hfin[:, :], hfin[:, :], fsq[:, kt % 2, :], ALU.add).then_inc(fin_sum, 1)
        vec.wait_ge(fin_mm, 1)
        fc = [0]

        def fin(ins):
            fc[0] += 1
            ins.then_inc(fin_c, 1)
            vec.wait_ge(fin_c, fc[0])

        fin(nc.vector.tensor_scalar(f2[:, :].rearrange(c2, c=2), ps[:, :, 0:HALF], EPS, None, ALU.add))
        fin(nc.vector.reciprocal(f3[:, :], f2[:, :]))
        vec.wait_ge(norm_sq, 4)
        fin(nc.vector.tensor_tensor(f3[:, :], f1[:, :], f1[:, :], ALU.mult))
        fin(nc.vector.tensor_tensor(f3[:, :], f3[:, :], f2[:, :], ALU.mult))
        fin(nc.vector.tensor_scalar(f3[:, :], f3[:, :], -0.5, 1.5, ALU.mult, ALU.add))
        fin(nc.vector.tensor_tensor(f1[:, :], f1[:, :], f3[:, :], ALU.mult))
        for kt in range(KT):
            nc.vector.scalar_tensor_tensor(out=xr[:, kt, :], in0=xr[:, kt, :], scalar=norms[:, 2, kt, 0:1],
                                           in1=f1[:, :], op0=ALU.mult, op1=ALU.mult).then_inc(fin_y, 1)

    with nc.Block() as block:
        @block.sync
        def _(sp):
            sync_program(sp)

        @block.gpsimd
        def _(pool):
            pool_program(pool)

        @block.tensor
        def _(pe):
            tensor_program(pe)

        @block.scalar
        def _(act):
            scalar_program(act)

        @block.vector
        def _(vec):
            vector_program(vec)


def laid_out(x):
    import numpy as np

    def f(v):
        return np.ascontiguousarray(v)

    def blocks(w, m=1):
        k, n = w.shape
        v = w.reshape(k // 128, 128, n // 128 // m, m, 128).transpose(2, 1, 3, 0, 4)
        return f(v).reshape(n // 128 // m, 128, -1)

    def per_channel(v):
        return f(np.asarray(v).reshape(-1, 128).T)

    w = {k: np.asarray(v) for k, v in x.items()}
    tok = np.concatenate([w["x_sample"][0], w["x_prompt"][0]], axis=0)
    o = {}
    o["x"] = f(tok.reshape(N, KT, 128).transpose(2, 1, 0))
    o["cond"] = f(np.stack([per_channel(w["c"][0]), per_channel(w["c_ctx"])], axis=2))
    o["w_ada"] = blocks(w["w_ada"][0])
    o["b_ada"] = per_channel(w["b_ada"][0])
    o["norms"] = f(np.stack([np.repeat(per_channel(g)[:, :, None], 2, axis=2)
                             for g in (w["norm1_g"][0], w["norm2_g"][0], w["final_norm_g"])], axis=1))
    win = blocks(w["w_in"][0])
    glu = 2 * CT
    q0, k0, v0, ga0 = glu, glu + NH, glu + NH + NKV, glu + NH + 2 * NKV
    order = [*range(v0, v0 + NKV), *range(k0, k0 + NKV), *range(q0, q0 + NH)]
    for m in range(CT):
        order += [CT + m, m]
    order += list(range(ga0, ga0 + 2 * KT))
    o["w_in"] = f(win[order])
    o["taps"] = f(w["conv_dw"][0].T.reshape(CT, 128, TAPS).transpose(1, 0, 2))
    o["convp"] = f(np.stack([per_channel(w[n][0]) for n in ("conv_dw_b", "conv_ln_g", "conv_ln_b")], axis=1))
    o["sinks"] = f(np.broadcast_to(w["attn_sink"][0][None], (128, NH)))
    o["cache_k"] = f(w["cache_k"][0, 0].transpose(1, 2, 0))
    o["cache_v"] = f(w["cache_v"][0, 0].reshape(2, 128, NKV, HD).transpose(2, 1, 0, 3))
    o["w_conv_out"] = blocks(w["w_conv_out"][0], 2)
    o["w_attn_out"] = blocks(w["w_attn_out"][0])
    o["w_out"] = blocks(w["w_out"][0])
    o["w_router"] = f(w["w_router"][0].reshape(KT, 128, NE).transpose(1, 0, 2))
    o["b_router"] = f(w["b_router"][0].reshape(NE, 1))
    gu = []
    for e in range(NE):
        g, u = blocks(w["w_exp_gate"][0, e]), blocks(w["w_exp_up"][0, e])
        gu.append(np.stack([g, u], axis=1).reshape(2 * FT, 128, -1))
    o["w_gu"] = f(np.concatenate(gu))
    o["w_exp_down"] = f(np.concatenate([blocks(w["w_exp_down"][0, e], 2) for e in range(NE)]))
    quarter = HD // 4
    inv = 10000.0 ** (-np.arange(quarter, dtype=np.float32) / np.float32(quarter))
    t = np.arange(NL)
    ang = [(p[None, :].astype(np.float32) * inv[:, None].astype(np.float32)).astype(np.float32)
           for p in (t // 64, t % 64)]
    cos, sin = np.ones((128, N), np.float32), np.zeros((128, N), np.float32)
    for b, an in enumerate(ang):
        for s in range(2):
            rows = slice(64 * b + 32 * s, 64 * b + 32 * s + 32)
            cos[rows, :NL] = np.cos(an)
            sin[rows, :NL] = np.sin(an) if s == 0 else -np.sin(an)
    o["cos"], o["sin"] = cos, sin
    q, k = np.arange(128)[:, None], np.arange(384)[None, :] - 128
    o["mask"] = np.where(np.abs(q - k) <= 128, 0.0, NEG).astype(np.float32)
    tri = (np.arange(128)[:, None] <= np.arange(128)[None, :]).astype(np.float32)
    o["triangle"] = f(np.stack([tri, np.ones((128, 128), np.float32)], axis=1))
    o["iota"] = np.broadcast_to(np.arange(1, 65, dtype=np.float32)[None], (128, 64)).copy()
    return o


def kernel(**inputs):
    import numpy as np
    import concourse.bacc as bacc
    from concourse.bass_utils import run_bass_kernel_spmd

    nc = bacc.Bacc("TRN2", target_bir_lowering=False, num_devices=1)
    host = laid_out(inputs)
    arrays, args = {}, {}
    for name, v in host.items():
        arrays[f"in_{name}"] = v
        args[name] = nc.dram_tensor(f"in_{name}", v.shape, F32, kind="ExternalInput").ap()
    outs = {"y": (KT, 128, N), "k": (NKV, 128, NC), "v": (NKV, 128, NC)}
    oaps = {n: nc.dram_tensor(f"out_{n}", s, F32, kind="ExternalOutput").ap() for n, s in outs.items()}
    build(nc, args, oaps)
    r = run_bass_kernel_spmd(nc, [arrays], core_ids=[0]).results[0]
    y = np.asarray(r["out_y"]).transpose(2, 0, 1).reshape(N, D)
    k = np.asarray(r["out_k"]).transpose(2, 0, 1)[None, None]
    v = np.asarray(r["out_v"]).transpose(2, 0, 1)[None, None]
    return (np.ascontiguousarray(y[NL:])[None], np.ascontiguousarray(y[:NL])[None],
            np.ascontiguousarray(k), np.ascontiguousarray(v))
```

```python
import concourse.bass as bass
from concourse import mybir
from concourse.alu_op_type import AluOpType as ALU

F32 = mybir.dt.float32
F32R = mybir.dt.float32r
ACT = mybir.ActivationFunctionType
AX = mybir.AxisListType.X
ds = bass.ds

D = 2048
KT = D // 128
NL = 512
NC = 128
N = NL + NC
PAST = 256
NH, NKV, HD = 16, 4, 128
GROUP = NH // NKV
CW = D // 2
CT = CW // 128
TAPS = 31
PAD = TAPS // 2
NE = 16
FT = (D // 2) // 128
CAPL, CAPC = 2 * NL // NE, 2 * NC // NE
CAP = CAPL + CAPC
EPS = 1e-6
SCALE = HD ** -0.5
NEG = -1e30
HALF = N // 2
ZW = PAD + NL + 2 * PAD + NC + PAD
CO = ZW - 2 * PAD
UNIT = 2048

RAW, SPL = 4, 2
A1, QN, GN, SN, TN, CN, ON = 2 * KT, 24, 16, 32, 16, 8, 16
ADA = 6 * KT
U = 4
US = 8
G_Q = A1
G_G = G_Q + QN
G_S = G_G + GN
G_T = G_S + 3 * SN
G_C = G_T + TN
G_O = G_C + CN
G_E = G_O + ON
CREDIT = SPL


SLOTS = 2 * CAP
LAT0 = (0, SLOTS - CAPL)
CTX0 = (CAPL, CAP)
AHEAD = 3
PHASES = (KT, KT, FT, FT)
PIECES = sum(PHASES)
BODIES = NE // 4
BODY_PIECES, BODY_SCATTERS, BODY_INNERS = 4 * PIECES, 4 * 2 * KT, 4 * 2
OLD_ITEMS = 7
BODY_TURNS = 2 * (4 + KT // 2 + 4)


class Step:

    def __init__(self):
        self.pair = self.piece = self.scatter = self.turn = self.turned = self.slots_done = self.inner = self.outer = 0
        self.what = None

    def now(self, *what):
        self.what = what
        return self


def raw_use(first, stride, body, i, k):
    at = first + stride * k
    return at % RAW, at // RAW + i * (body * stride // RAW)


def build(nc, a, out):
    def sem(name):
        return nc.alloc_semaphore(name)

    base = 16512
    X0 = base
    R0 = X0 + 2 * KT * N * 4
    S0 = R0 + RAW * UNIT * 4
    Y0 = S0 + 2 * SPL * UNIT * 4
    Z0 = 229344

    names = {}

    def at(name, shape, dtype, offset):
        offset = (offset + 31) // 32 * 32
        names[name] = nc.alloc_sbuf_tensor_at(name, shape, dtype, offset=offset)
        size = 4
        for x in shape[1:]:
            size *= x
        assert offset + size <= Z0, (name, offset + size)
        return names[name], offset + size

    hhi, o = at("hhi", [128, KT, N], F32R, X0)
    hlo, o = at("hlo", [128, KT, N], F32R, o)
    raw, o = at("raw", [128, RAW, UNIT], F32, R0)
    whi, o = at("whi", [128, SPL, UNIT], F32R, S0)
    wlo, o = at("wlo", [128, SPL, UNIT], F32R, o)

    o = Z0 - 4800
    SMALL = o
    mod, o = at("mod", [128, ADA, 2], F32, o)
    bada, o = at("bada", [128, ADA], F32, o)
    cond, o = at("cond", [128, KT, 2], F32, o)
    norms, o = at("norms", [128, 3, KT, 2], F32, o)
    gsc, o = at("gsc", [128, KT, 2], F32, o)
    ghalf, o = at("ghalf", [128, KT, 2], F32, o)
    taps, o = at("taps", [128, CT, TAPS], F32, o)
    convp, o = at("convp", [128, 3, CT], F32, o)
    sinks, o = at("sinks", [128, NH], F32, o)
    negsink, o = at("negsink", [128, NH], F32, o)
    ident, o = at("ident", [128, 128], F32, o)
    ones, o = at("ones", [128, 128], F32, o)
    mx, o = at("mx", [128, 2], F32, o)
    nm, o = at("nm", [128, 1], F32, o)
    dn, o = at("dn", [128, 3], F32, o)
    rd, o = at("rd", [128, 2], F32, o)
    brt, o = at("brt", [16, 1], F32, o)
    gates, o = at("gates", [128, 4], F32, o)

    row4, _ = at("row4", [128, RAW, 128], F32, X0)
    row1, _ = at("row1", [128, 128], F32, SMALL - 512)
    xin, o = at("xin", [128, KT, N], F32, Y0)
    t1, o = at("t1", [128, N], F32, o)
    t2, o = at("t2", [128, N], F32, o)
    t3, o = at("t3", [128, N], F32, o)
    t4, o = at("t4", [128, N], F32, o)
    rstd, o = at("rstd", [128, N], F32, o)
    assert o <= SMALL - 512

    zt, o = at("zt", [128, CT, ZW], F32, Y0)
    ctmp, o = at("ctmp", [128, CO], F32, o)
    ktg, o = at("ktg", [128, N + PAST], F32, o)
    vg, o = at("vg", [128, (N + PAST) // 128, HD], F32, o)
    qh, o = at("qh", [128, 2, N], F32, o)
    sm, o = at("sm", [128, 384], F32, o)
    pe_, o = at("pexp", [128, 640], F32, o)
    pn, o = at("pn", [128, 640], F32, o)
    pt_sb, o = at("pt_sb", [128, 640], F32, o)
    ao, o = at("ao", [128, 2, 128], F32, o)
    th, o = at("th", [128, 2, N], F32, o)
    mask, o = at("mask", [128, 384], F32, o)
    assert o <= SMALL - 512, (o, SMALL)
    cost, o = at("cost", [128, N], F32, Y0)
    sint, o = at("sint", [128, N], F32, o)
    ra, o = at("ra", [128, N], F32, o)
    rb, o = at("rb", [128, N], F32, o)
    rbs, o = at("rbs", [128, N], F32, o)
    ro, o = at("ro", [128, N], F32, o)
    vst, o = at("vst", [128, N], F32, o)
    vtk, o = at("vtk", [128, N], F32, o)
    assert o <= Y0 + CT * ZW * 4
    gsig, o = at("gsig", [128, N], F32, Y0 + CT * ZW * 4)

    alo, o = at("alo", [128, CT, N], F32R, Y0)
    ahi, o = at("ahi", [128, CT, N], F32R, Y0 + CT * ZW * 4)
    gl, o = at("gl", [128, 2, N], F32, o)
    att4, _ = at("att4", [128, 4, N], F32, o - 2 * N * 4)
    mo, o = at("mo", [128, 2, N], F32, o)
    lt1, o = at("lt1", [128, N], F32, o)
    lt2, o = at("lt2", [128, N], F32, o)
    assert o <= SMALL - 512, (o, SMALL)
    ls1, _ = at("ls1", [128, 672], F32, Y0 + CT * ZW * 4)
    ls2, _ = at("ls2", [128, 672], F32, Y0 + CT * ZW * 4 + 2688)
    ls3, _ = at("ls3", [128, 672], F32, Y0 + CT * ZW * 4 + 2 * 2688)
    lq, _ = at("lq", [128, 2, 672], F32, Y0 + CT * ZW * 4 + 3 * 2688)

    xr, o = at("xr", [128, KT, N], F32, Y0)
    YE = o
    sq, o = at("sq", [128, N], F32, YE)
    ssum, o = at("ssum", [128, N], F32, o)
    e1, o = at("e1", [128, N], F32, o)
    e2, o = at("e2", [128, N], F32, o)
    e3, o = at("e3", [128, N], F32, o)
    h2t, o = at("h2t", [128, 1, N], F32, o)
    assert o <= SMALL - 512, (o, SMALL)
    h2, o = at("h2", [128, 5, D], F32, X0)
    xhi, o = at("xhi", [128, 2, KT, SLOTS], F32R, o)
    xlo, o = at("xlo", [128, 2, KT, SLOTS], F32R, o)
    assert o <= R0
    ehi, o = at("ehi", [128, AHEAD, 1024], F32R, S0)
    elo, o = at("elo", [128, AHEAD, 1024], F32R, o)
    hthi, o = at("hthi", [128, FT, 128], F32R, o)
    zeros, _ = at("zeros", [128, 1024], F32, o)
    htlo, o = at("htlo", [128, FT, 128], F32R, o)
    assert o <= Y0, (o, Y0)
    yhi, o = at("yhi", [128, 1024], F32R, YE)
    ylo, o = at("ylo", [128, 1024], F32R, o)
    oht, o = at("oht", [128, 2, N], F32R, o)
    oh, o = at("oh", [128, 5, SLOTS], F32, o)
    PW = o
    wr, _ = at("wr", [128, KT, NE], F32, S0)
    lgT, o = at("lgT", [16, N], F32, S0 + 1024)
    work, o = at("work", [16, N], F32, o)
    affT, o = at("affT", [16, N], F32, o)
    top8, o = at("top8", [16, 8], F32, o)
    sm5, o = at("sm5", [128, 5, NE], F32, o)
    sm5b, o = at("sm5b", [128, 5], F32, o)
    trio, o = at("trio", [128, 2, 128], F32, o)
    mk5, o = at("mk5", [128, 5, NE], F32, o)
    aff, o = at("aff", [128, 5, NE + 2], F32, PW)
    posm, o = at("posm", [128, 5, NE + 2], F32, o)
    iota, o = at("iota", [128, 64], F32, o)
    own, o = at("own", [128, 2], F32, o)
    hid, o = at("hid", [128, 512], F32, o)
    assert o <= SMALL, (o, SMALL)

    pu = nc.alloc_psum_tensor("pu", [128, 4, 512], F32)
    ps = nc.alloc_psum_tensor("ps", [128, 2, 512], F32)
    pt = nc.alloc_psum_tensor("pt", [128, 2, 512], F32)

    def dr(name, shape):
        return nc.dram_tensor(name, shape, F32).ap()

    qT_d, kT_d = dr("q_rot", [NH, 128, N]), dr("k_rot", [NKV, 128, N])
    v_d = dr("v_tok", [NKV, 128, 5, HD])
    at_d = dr("att", [NH, 128, N])
    th_d = dr("gates_tanh", [2 * KT, 128, N])
    mx_d = dr("mixed_a", [KT, 128, N])

    raw_loaded = [sem(f"raw_loaded{i}") for i in range(RAW)]
    raw_freed = [sem(f"raw_freed{i}") for i in range(RAW)]
    hi_ready, lo_ready = sem("hi_ready"), sem("lo_ready")
    dense_mm = sem("dense_mm")
    psum_free = [sem("psum_free0"), sem("psum_free1")]
    ada_read = sem("ada_read")
    ada_turned, mod_ready = sem("ada_turned"), sem("mod_ready")
    small_loaded = sem("small_loaded")
    x_loaded = [sem(f"x_loaded{i}") for i in range(4)]
    const_made = sem("const_made")
    cond_ready = sem("cond_ready")
    sq_made, sq_summed = sem("sq_made"), sem("sq_summed")
    norm_mm, norm_t, norm_sq = sem("norm_mm"), sem("norm_t"), sem("norm_sqrt")
    vec_done = sem("vec_done")
    act_done = sem("act_done")
    gsc_ready = sem("gsc_ready")
    xn_ready = sem("xn_ready")
    h_hi, h_lo = sem("h_hi"), sem("h_lo")
    tabs_loaded = sem("tabs_loaded")
    rope_b, rope_swapped, rope_out, rope_stored = sem("rope_b"), sem("rope_swapped"), sem("rope_out"), sem("rope_stored")
    rope_a = sem("rope_a")
    v_read, v_tr, v_tok, v_stored, vx_stored = sem("v_read"), sem("v_tr"), sem("v_tok"), sem("v_stored"), sem("vx_stored")
    glu_sig, glu_z = sem("glu_sig"), sem("glu_z")
    z_zero = sem("z_zero")
    values_loaded = sem("values_loaded")
    kv_loaded, q_loaded = sem("kv_loaded"), [sem("q_loaded0"), sem("q_loaded1")]
    att_qk, att_nm, att_exp, att_pn = sem("att_qk"), sem("att_nm"), sem("att_exp"), sem("att_pn")
    att_tr, att_pt, att_pv, att_out = sem("att_tr"), sem("att_pt"), sem("att_pv"), sem("att_out")
    att_v = sem("att_v")
    att_stored = [sem("att_stored0"), sem("att_stored1")]
    conv_done = sem("conv_done")
    th_ready, th_stored = sem("th_ready"), [sem("th_stored0"), sem("th_stored1")]
    attn_loaded, attn_hi, attn_lo = [sem(f"attn_loaded{i}") for i in range(4)], sem("attn_hi"), sem("attn_lo")
    gl_loaded = [sem("gl_loaded0"), sem("gl_loaded1")]
    mo_ready, mo_stored = sem("mo_ready"), [sem("mo_stored0"), sem("mo_stored1")]
    ln_sum, ln_mm, ln_sq, ln_c = sem("ln_sum"), sem("ln_mm"), sem("ln_sq"), sem("ln_c")
    ln_act, ln_hi, ln_lo = sem("ln_act"), sem("ln_hi"), sem("ln_lo")
    ml_loaded = [sem("ml_loaded0"), sem("ml_loaded1")]
    mix_sum, mix_hi, mix_lo = sem("mix_sum"), sem("mix_hi"), sem("mix_lo")
    xr_loaded = sem("xr_loaded")
    res_done, res_sq, res_sum = sem("res_done"), sem("res_sq"), sem("res_sum")
    h2_vec, h2_act, h2_tr, h2_hi, h2_lo, h2_mm = (sem("h2_vec"), sem("h2_act"), sem("h2_tr"), sem("h2_hi"),
                                                  sem("h2_lo"), sem("h2_mm"))
    rt_loaded = sem("rt_loaded")
    rt_pe, rt_vec, rt_act = sem("rt_pe"), sem("rt_vec"), sem("rt_act")
    sel_made = sem("sel_made")
    psu_mm, psu_hi, psu_lo = sem("psu_mm"), sem("psu_hi"), sem("psu_lo")
    ex_hi, ex_lo, ex_mm = sem("ex_hi"), sem("ex_lo"), sem("ex_mm")
    hid_silu, hid_done = sem("hid_silu"), sem("hid_done")
    y_hi, y_lo = sem("y_hi"), sem("y_lo")
    sc_mm, sc_add = sem("sc_mm"), sem("sc_add")
    fin_sq, fin_sum, fin_mm, fin_c, fin_y, fin_stored = (sem("fin_sq"), sem("fin_sum"), sem("fin_mm"), sem("fin_c"),
                                                         sem("fin_y"), sem("fin_stored"))
    states_stored = sem("states_stored")
    pool_passed, vec_passed = sem("pool_passed"), sem("vec_passed")

    SEGS = [(0, 0, 0, HALF), (HALF, 1, 0, NL - HALF), (NL, 1, NL - HALF, HALF)]

    def att_steps():
        return [(h, j) for h in range(GROUP) for j in range(NL // 128 + 1)]

    STEPS = att_steps()
    NS = len(STEPS)
    CUT = [NS * k // US for k in range(US + 1)]

    def body_steps():
        gathers = [(0, 1, 15), (0, 2, 1), (0, 2, 4), (0, 2, 6), (1, 1, 11), (1, 1, 14), (1, 2, 1), (1, 2, 5)]
        old_first, old_second = (1,) * 9, (0,) * 10 + (1,) * 16
        new_first = (0, 0, 1, 1, 1, 1, 1, 2)
        at_ = Step()
        for pair in range(2):
            at_.pair = pair
            for x in range(2):
                for h in range(4):
                    for k in range(PHASES[h]):
                        yield at_.now("piece", x, h, k)
                        at_.piece += 1
                        at_k = k + (KT if h == 1 else 0)
                        items = [(1 - x, 0)] * (old_first[at_k] if h < 2 and at_k < len(old_first) else 0)
                        items += [(1 - x, 1)] * (old_second[at_k] if h < 2 and at_k < len(old_second) else 0)
                        items += [(x, 0)] * (new_first[k] if h == 3 else 0)
                        for whose, half in items:
                            yield at_.now("scatter", whose, half, (at_.scatter + OLD_ITEMS) % 16)
                            at_.scatter += 1
                        if (h, k) == (0, len(old_first) - 1):
                            yield at_.now("outer", 1 - x, 1, 0)
                            at_.outer += 1
                        if (x, h) == (0, 1) and 10 <= k < 14:
                            yield at_.now("slots", (k - 10) // 2, (k - 10) % 2, 0)
                            at_.turn += 1
                            at_.slots_done = at_.turn
                            if k == 13:
                                yield at_.now("select", 0, 0, 0)
                        if (x, h, k) in gathers:
                            yield at_.now("gather", 0, 0, gathers.index((x, h, k)))
                            at_.turn += 1
                        if (h, k) in ((1, 4), (2, 2)):
                            yield at_.now("turn", x, h - 1, 0)
                            at_.turn += 1
                            at_.turned = at_.turn
                    if h < 2:
                        yield at_.now("inner", x, h, 0)
                        at_.inner += 1
                    elif h == 2:
                        yield at_.now("outer", x, 0, 0)
                        at_.outer += 1

    def keys_of(j):
        lo, hi = max(0, j - 1), min(NL // 128, j + 2)
        return lo, hi

    def sync_program(sp):
        def load(src, slot, use, first=False):
            if not first:
                sp.wait_ge(raw_freed[slot], 2 * use)
            sp.dma_start(raw[:, slot, :], src).then_inc(raw_loaded[slot], 16)

        for k in range(RAW):
            load(a["w_ada"][k], k, 0, first=True)
        with sp.Fori(1, A1 // RAW) as i:
            for k in range(RAW):
                load(a["w_ada"][i * RAW + k], *raw_use(0, 1, RAW, i, k))
        with sp.Fori(0, (QN + GN) // U) as i:
            for k in range(U):
                load(a["w_in"][i * U + k], *raw_use(G_Q, 1, U, i, k))
        with sp.Fori(0, SN // US) as i:
            for k in range(US):
                slot, use = raw_use(G_S, 3, US, i, k)
                load(a["w_in"][i * US + (QN + GN + k)], slot, use)
                for b in range(2):
                    at_ = G_S + 3 * k + 1 + b
                    load(a["w_ada"][i * (2 * US) + (A1 + 2 * k + b)], at_ % RAW, at_ // RAW + i * (3 * US // RAW))
        for name, first, n in (("w_attn_out", G_T, TN), ("w_conv_out", G_C, CN), ("w_out", G_O, ON)):
            with sp.Fori(0, n // U) as i:
                for k in range(U):
                    load(a[name][i * U + k], *raw_use(first, 1, U, i, k))
        per = PIECES // 2
        with sp.Fori(0, NE) as e:
            for k in range(per):
                load(a["w_experts"][e * per + k], *raw_use(G_E, 1, per, e, k))

    def pool_program(pool):
        def settle():
            pool.sem_inc(pool_passed, 1)

        pool.memset(ident[:, :], 0.0).then_inc(const_made, 1)
        pool.memset(ones[:, :], 1.0 / D).then_inc(const_made, 1)
        pool.wait_ge(const_made, 2)
        pool.affine_select(out=ident[:, :], in_=ident[:, :], compare_op=ALU.not_equal, fill=1.0, base=0,
                           pattern=[[-1, 128]], channel_multiplier=1).then_inc(const_made, 1)
        for dst, name in ((cond, "cond"), (bada, "b_ada"), (norms, "norms"), (taps, "taps"), (convp, "convp"),
                          (sinks, "sinks")):
            pool.dma_start(dst[:], a[name]).then_inc(small_loaded, 16)
        pool.dma_start(brt[:, :], a["b_router"]).then_inc(small_loaded, 16)
        for c in range(4):
            pool.dma_start(xin[:, 4 * c:4 * c + 4, :], a["x"][:, 4 * c:4 * c + 4, :]).then_inc(x_loaded[c], 16)
        pool.wait_ge(h_lo, KT)
        pool.dma_start(cost[:, :], a["cos"]).then_inc(tabs_loaded, 16)
        pool.dma_start(sint[:, :], a["sin"]).then_inc(tabs_loaded, 16)
        pool.dma_start(mask[:, :], a["mask"]).then_inc(tabs_loaded, 16)

        def store_v(n):
            pool.wait_ge(v_read, n + 1)
            pool.dma_start(out["v"][n], vst[:, NL:N]).then_inc(vx_stored, 16)
            pool.wait_ge(v_tok, n + 1)
            pool.dma_start(v_d[n], vtk[:, :].rearrange("p (t d) -> p t d", d=HD)).then_inc(v_stored, 16)

        def rotate(n, dst, state=None):
            pool.wait_ge(rope_b, n + 1)
            settle()
            for q in range(4):
                s = q ^ 1
                pool.dma_start(rbs[32 * q:32 * q + 32, :], rb[32 * s:32 * s + 32, :]).then_inc(rope_swapped, 16)
            pool.wait_ge(rope_out, n + 1 + 1)
            settle()
            pool.dma_start(dst, ro[:, :]).then_inc(rope_stored, 16)
            if state is not None:
                pool.dma_start(state, ro[:, NL:N]).then_inc(rope_stored, 16)

        for n in range(NKV):
            store_v(n)
        for n in range(NKV):
            rotate(n, kT_d[n], out["k"][n])
        with pool.Fori(0, NH) as n:
            rotate(n + NKV, qT_d[n])

        def load_group(i):
            pool.wait_ge(rope_stored, 16 * (2 * NKV + NH))
            pool.wait_ge(v_stored, 16 * NKV)
            load_q(i, 0)
            pool.wait_ge(att_qk, NS * i + 10)
            settle()
            pool.dma_start(ktg[:, 0:N], kT_d[i]).then_inc(kv_loaded, 16)
            pool.dma_start(ktg[:, N:N + PAST], a["cache_k"][i]).then_inc(kv_loaded, 16)
            pool.wait_ge(att_pv, NS * i + 1)
            settle()
            pool.dma_start(vg[:, 0:5, :], v_d[i]).then_inc(values_loaded, 16)
            pool.dma_start(vg[:, 5:7, :], a["cache_v"][i]).then_inc(values_loaded, 16)

        def load_q(i, h):
            pool.wait_ge(att_qk, NS * i + 5 * h + 5)
            settle()
            pool.dma_start(qh[:, h % 2, :], qT_d[i * GROUP + h]).then_inc(q_loaded[h % 2], 16)

        with pool.Fori(0, NKV) as i:
            load_group(i)
            load_q(i, 1)
            for k in range(US):
                for n in range(CUT[k], CUT[k + 1]):
                    h, j = STEPS[n]
                    if j == 0 and 0 < h and h + 1 < GROUP:
                        load_q(i, h + 1)
                    pool.wait_ge(att_out, i * NS + (n + 1) + 1)
                    settle()
                    pool.dma_start(at_d[i * GROUP + h][:, 128 * j:128 * j + 128],
                                   ao[:, n % 2, :]).then_inc(att_stored[n % 2], 16)
                pool.wait_ge(th_ready, i * US + (k + 1))
                settle()
                pool.dma_start(th_d[i * US + k], th[:, k % 2, :]).then_inc(th_stored[k % 2], 16)

        for b in range(2):
            pool.wait_ge(att_stored[b], 16 * (NKV * NS // 2))
            pool.wait_ge(th_stored[b], 16 * (SN // 2))

        def gate_load(m, which):
            pool.dma_start(gl[:, m % 2, :], th_d[which * KT + m]).then_inc(gl_loaded[m % 2], 16)

        for m in range(KT):
            if m >= 4:
                pool.wait_ge(attn_lo, m - 3)
            pool.dma_start(att4[:, m % 4, :], at_d[m]).then_inc(attn_loaded[m % 4], 16)
        pool.wait_ge(attn_lo, KT)
        for m in range(2):
            gate_load(m, 1)
        for m in range(KT):
            pool.wait_ge(mo_ready, m + 1)
            pool.dma_start(mx_d[m], mo[:, m % 2, :]).then_inc(mo_stored[m % 2], 16)
            if m + 2 < KT:
                gate_load(m + 2, 1)
        for b in range(2):
            pool.wait_ge(mo_stored[b], 16 * (KT // 2))
        for m in range(KT):
            if m >= 2:
                pool.wait_ge(mix_sum, m - 1)
            gate_load(m, 0)
            pool.dma_start(mo[:, m % 2, :], mx_d[m]).then_inc(ml_loaded[m % 2], 16)
        pool.wait_ge(dense_mm, CREDIT + QN + GN + SN + TN + 2 * CN)
        for c in range(4):
            pool.dma_start(xr[:, 4 * c:4 * c + 4, :], a["x"][:, 4 * c:4 * c + 4, :]).then_inc(xr_loaded, 16)
        pool.wait_ge(dense_mm, CREDIT + QN + GN + SN + TN + 2 * CN + ON)
        pool.dma_start(wr[:, :, :], a["w_router"]).then_inc(rt_loaded, 16)
        pool.dma_start(trio[:, :, :], a["triangle"]).then_inc(rt_loaded, 16)
        pool.dma_start(iota[:, :], a["iota"]).then_inc(rt_loaded, 16)
        pool.dma_start(own[:, :], a["own"]).then_inc(rt_loaded, 16)
        with pool.Fori(0, KT) as m:
            pool.wait_ge(fin_y, m + 1)
            settle()
            pool.dma_start(out["y"][m], xr[:, ds(m, 1), :].rearrange("p a n -> p (a n)")).then_inc(fin_stored, 16)
        pool.wait_ge(fin_stored, 16 * KT)
        pool.wait_ge(vx_stored, 16 * NKV)
        pool.wait_ge(rope_stored, 16 * (2 * NKV + NH))

    def norm_chain(vec, act_side, step, total, mean, t, r, w1, w2, width):
        n = total

        def did(ins):
            nonlocal n
            ins.then_inc(step, 1)
            n += 1
            vec.wait_ge(step, n)

        did(nc.vector.tensor_scalar(t, mean, EPS, None, ALU.add))
        did(nc.vector.reciprocal(w1, t))
        act_side(n)
        did(nc.vector.tensor_tensor(w2, r, r, ALU.mult))
        did(nc.vector.tensor_tensor(w2, w2, t, ALU.mult))
        did(nc.vector.tensor_scalar(w2, w2, -0.5, 1.5, ALU.mult, ALU.add))
        did(nc.vector.tensor_tensor(r, r, w2, ALU.mult))
        return n

    def tensor_program(pe):
        def ada_unit(slot, use, read, bank, row):
            pe.wait_ge(raw_loaded[slot], 16 * (use + 1))
            pe.wait_ge(ada_read, read)
            for kt in range(KT):
                last = nc.tensor.matmul(bank[0:2, 0:128], cond[:, kt, :], raw[:, slot, kt * 128:kt * 128 + 128],
                                        start=kt == 0, stop=kt == KT - 1)
            if row is not None:
                last = nc.tensor.transpose(bank[:, 128:130], row, ident[0:2, 0:2])
            last.then_inc(raw_freed[slot], 2)

        def dense(d, p, dk, pk, hi, lo, k0, k1, off, kts):
            for kt in range(k0, k1):
                w = off + kt * 128
                for c in range(2):
                    o = pu[:, 2 * pk + c, 0:HALF]
                    cols = slice(c * HALF, c * HALF + HALF)
                    nc.tensor.matmul(o, whi[:, dk, w:w + 128], hi[:, kt, cols], start=kt == 0, stop=False)
                    nc.tensor.matmul(o, whi[:, dk, w:w + 128], lo[:, kt, cols], start=False, stop=False)
                    last = nc.tensor.matmul(o, wlo[:, dk, w:w + 128], hi[:, kt, cols], start=False,
                                            stop=kt == kts - 1)
            if k1 == kts:
                last.then_inc(dense_mm, 1)

        def dense_start(d, p, i=0, body=0):
            pe.wait_ge(hi_ready, d + 1)
            pe.wait_ge(lo_ready, d + 1)
            pe.wait_ge(psum_free[p % 2], i * (body // 2) + (p // 2 + 1))

        def mean_over_channels(src, dst, width, signal):
            for c in range(2):
                last = nc.tensor.matmul(dst[:, c, 0:width], ones[:, :], src[:, c * width:(c + 1) * width],
                                        start=True, stop=True)
            last.then_inc(signal, 1)

        pe.sem_inc(dense_mm, CREDIT)
        pe.sem_inc(att_qk, 10)
        pe.sem_inc(att_pv, 1)
        pe.sem_inc(att_tr, 1)
        pe.wait_ge(const_made, 3)
        pe.wait_ge(cond_ready, 1)
        for k in range(RAW):
            ada_unit(*raw_use(0, 1, RAW, 0, k), k + 1, pu[:, k, :], None)
        pe.wait_ge(sq_summed, KT)
        mean_over_channels(t1, ps, HALF, norm_mm)
        with pe.Fori(1, A1 // RAW) as i:
            for k in range(RAW):
                ada_unit(*raw_use(0, 1, RAW, i, k), i * RAW + k + 1, pu[:, k, :], row4[0:2, k, :])
        pe.wait_ge(ada_read, RAW + A1)
        for k in range(RAW):
            last = nc.tensor.transpose(pu[:, k, 128:130], row4[0:2, k, :], ident[0:2, 0:2])
        last.then_inc(ada_turned, 1)
        pe.wait_ge(mod_ready, 1)
        for d in range(2 * NKV):
            dense_start(d, d)
            for kt in range(KT):
                if d == 0:
                    pe.wait_ge(h_hi, kt + 1)
                    pe.wait_ge(h_lo, kt + 1)
                dense(d, d, d % 2, d % 2, hhi, hlo, kt, kt + 1, 0, KT)
            if 1 <= d <= NKV:
                n = d - 1
                pe.wait_ge(v_read, n + 1)
                if n:
                    pe.wait_ge(v_tok, n)
                for t in range(5):
                    last = nc.tensor.transpose(pt[:, t // 4, 128 * (t % 4):128 * (t % 4) + 128],
                                               vst[:, 128 * t:128 * t + 128], ident[:, :])
                last.then_inc(v_tr, 1)
        with pe.Fori(2 * NKV // U, (QN + GN) // U) as i:
            for k in range(U):
                d = i * U + k
                dense_start(d, k, i, U)
                dense(d, d, k % 2, k % 2, hhi, hlo, 0, KT, 0, KT)

        def qk(i, n):
            h, j = STEPS[n]
            if n == 0:
                pe.wait_ge(kv_loaded, i * 32 + 32)
            if j == 0:
                uses = 2
                pe.wait_ge(q_loaded[h % 2], (i * uses + (h // 2 + 1)) * 16)
            pe.wait_ge(att_exp, i * NS + n + 1)
            pe.wait_ge(att_pt, i * NS + n + 1)
            qb = qh[:, h % 2, 128 * j:128 * j + 128]
            if j < NL // 128:
                lo, hi = keys_of(j)
                nc.tensor.matmul(ps[:, 0, 0:128 * (hi - lo)], qb, ktg[:, 128 * lo:128 * hi], start=True, stop=True)
                last = nc.tensor.matmul(ps[:, 1, 0:PAST], qb, ktg[:, N:N + PAST], start=True, stop=True)
            else:
                last = nc.tensor.matmul(ps[:, 0, 0:NC], qb, ktg[:, NL:N], start=True, stop=True)
            last.then_inc(att_qk, 1)

        def turn(i, n):
            h, j = STEPS[n]
            lo, hi = keys_of(j)
            blocks = hi - lo + 2 if j < 4 else 1
            pe.wait_ge(att_pn, i * NS + (n + 1))
            pe.wait_ge(att_out, i * NS + n + 1)
            for b in range(blocks):
                last = nc.tensor.transpose(pt[:, 0, 128 * b:128 * b + 128] if b < 4 else ps[:, 1, 0:128],
                                           pn[:, 128 * b:128 * b + 128], ident[:, :])
            last.then_inc(att_tr, 1)

        def pv(i, n):
            h, j = STEPS[n]
            lo, hi = keys_of(j)
            vs = [*range(lo, hi), 5, 6] if j < 4 else [4]
            if n == 0:
                pe.wait_ge(values_loaded, i * 32 + 32)
            pe.wait_ge(att_pt, i * NS + (n + 1) + 1)
            for b, v in enumerate(vs):
                last = nc.tensor.matmul(pt[:, 0, 0:128], vg[:, v, :], pt_sb[:, 128 * b:128 * b + 128],
                                        start=b == 0, stop=b == len(vs) - 1)
            last.then_inc(att_pv, 1)

        with pe.Fori(0, SN // US) as i:
            for k in range(US):
                d = i * US + (QN + GN + k)
                dense_start(d, QN + GN + k, i, US)
                steps = list(range(CUT[k], CUT[k + 1]))
                cuts = [KT * x // len(steps) for x in range(len(steps) + 1)]
                for x, n in enumerate(steps):
                    qk(i, n)
                    dense(d, d, k % 2, k % 2, hhi, hlo, cuts[x], cuts[x + 1], 0, KT)
                    turn(i, n)
                    if x < 2:
                        at_ = G_S + 3 * k + 1 + x
                        ada_unit(at_ % RAW, at_ // RAW + i * (3 * US // RAW),
                                 i * (2 * US) + (RAW + A1 + 2 * k + x), pt[:, 1, :], row1[0:2, :])
                    pv(i, n)
        pe.wait_ge(ada_read, RAW + ADA)
        nc.tensor.transpose(pt[:, 1, 128:130], row1[0:2, :], ident[0:2, 0:2]).then_inc(ada_turned, 1)

        D_T = QN + GN + SN
        for t in range(TN):
            d = D_T + t
            dense_start(d, d)
            for kt in range(KT):
                if t == 0:
                    pe.wait_ge(attn_hi, kt + 1)
                    pe.wait_ge(attn_lo, kt + 1)
                dense(d, d, t % 2, t % 2, hhi, hlo, kt, kt + 1, 0, KT)
            if t == 1:
                pe.wait_ge(ln_sum, 1)
                mean_over_channels(ls1, ps, CO // 2, ln_mm)
            if t == 3:
                pe.wait_ge(ln_sum, 2)
                mean_over_channels(ls1, pt, CO // 2, ln_mm)
        pe.wait_ge(ln_hi, CT)
        pe.wait_ge(ln_lo, CT)
        for c in range(CN):
            for b in range(2):
                d, p = D_T + TN + c, D_T + TN + 2 * c + b
                dense_start(d, p)
                dense(d, p, c % 2, b, ahi, alo, 0, CT, b * CT * 128, CT)
        pe.wait_ge(mix_hi, KT)
        pe.wait_ge(mix_lo, KT)
        with pe.Fori(0, ON // U) as i:
            for k in range(U):
                d = i * U + (D_T + TN + CN + k)
                p = D_T + TN + 2 * CN + k
                dense_start(d, p, i, U)
                dense(d, p, k % 2, k % 2, hhi, hlo, 0, KT, 0, KT)

        pe.wait_ge(res_sum, KT)
        mean_over_channels(ssum, ps, HALF, norm_mm)
        pe.wait_ge(rt_loaded, 64)
        for kt in range(KT):
            pe.wait_ge(h2_act, kt + 1)
            nc.tensor.matmul(ps[0:16, 0, :], wr[:, kt, :], h2t[:, 0, 0:NL], start=kt == 0, stop=kt == KT - 1)
            nc.tensor.matmul(ps[0:16, 1, 0:NC], wr[:, kt, :], h2t[:, 0, NL:N], start=kt == 0, stop=kt == KT - 1)
            if kt >= 2:
                pe.wait_ge(h2_hi, kt - 1)
            for t in range(5):
                last = nc.tensor.transpose(pu[:, 2 * (kt % 2) + t // 4, 128 * (t % 4):128 * (t % 4) + 128],
                                           h2t[:, 0, 128 * t:128 * t + 128], ident[:, :])
            last.then_inc(h2_tr, 1)
        pe.wait_ge(rt_act, 1)
        for t in range(5):
            last = nc.tensor.transpose(pt[:, 0, NE * t:NE * t + NE], lgT[:, 128 * t:128 * t + 128],
                                       ident[0:16, 0:16])
        last.then_inc(rt_pe, 1)
        pe.wait_ge(rt_vec, RV_AFF)
        for t in range(5):
            last = nc.tensor.transpose(ps[0:16, t // 4, 128 * (t % 4):128 * (t % 4) + 128], aff[:, t, 0:NE],
                                       ident[:, :])
        last.then_inc(rt_pe, 1)
        pe.wait_ge(rt_vec, RV_MASK)
        for t in range(5):
            last = nc.tensor.transpose(pt[:, 0, NE * t:NE * t + NE], work[:, 128 * t:128 * t + 128],
                                       ident[0:16, 0:16])
        last.then_inc(rt_pe, 1)
        pe.wait_ge(rt_vec, RV_MK5)
        for t in range(5):
            first = 0 if t < 4 else 4
            for s in range(first, t + 1):
                last = nc.tensor.matmul(pt[:, 1, NE * t:NE * t + NE], trio[:, 0 if s == t else 1, :], mk5[:, s, :],
                                        start=s == first, stop=s == t)
        last.then_inc(rt_pe, 1)

        def gather(g, ready, bank, u):
            pe.wait_ge(sel_made, ready)
            pe.wait_ge(psu_lo, u + 1)
            for kt in (2 * g, 2 * g + 1):
                o = ps[:, bank, SLOTS * (kt % 2):SLOTS * (kt % 2) + SLOTS]
                for t in range(5):
                    last = nc.tensor.matmul(o, h2[:, t, kt * 128:kt * 128 + 128], oh[:, t, :], start=t == 0,
                                            stop=t == 4)
            last.then_inc(psu_mm, 1)

        def scatter(m, c, x, y_count, s):
            if k_first(m, c):
                pe.wait_ge(y_lo, y_count)
            pe.wait_ge(sc_add, s + 1)
            cols = slice(128 * (m % 8), 128 * (m % 8) + 128)
            toks = slice(HALF * c, HALF * c + HALF)
            nc.tensor.matmul(pt[:, c, 0:HALF], yhi[:, cols], oht[:, x, toks], start=True, stop=False)
            nc.tensor.matmul(pt[:, c, 0:HALF], ylo[:, cols], oht[:, x, toks], start=False,
                             stop=True).then_inc(sc_mm, 1)

        def k_first(m, c):
            return m % 8 == 0 and c == 0

        pe.wait_ge(rt_vec, RV_END)
        for g in range(KT // 2):
            gather(g, 1, g % 2, g)
        with pe.Fori(0, BODIES) as i:
            for st in body_steps():
                kind, x, h, k = st.what
                if kind == "piece":
                    n = i * BODY_PIECES + st.piece
                    if h == 0 and k == 0:
                        pe.wait_ge(psu_lo, i * BODY_TURNS + (KT // 2 + st.turn + 2))
                    pe.wait_ge(ex_hi, n + 1)
                    pe.wait_ge(ex_lo, n + 1)
                    if h < 2:
                        hi, lo = (v[:, st.pair % 2, k, 32 * x:32 * x + 128] for v in (xhi, xlo))
                    else:
                        if h == 2 and k in (0, 4):
                            pe.wait_ge(psu_lo, i * BODY_TURNS + (KT // 2 + st.turned + 2))
                        hi, lo = hthi[:, k, :], htlo[:, k, :]
                    slot, end = st.piece % 3, k == PHASES[h] - 1
                    for left, ring in ((hi, ehi), (hi, elo), (lo, ehi)):
                        for c in range(2):
                            last = nc.tensor.matmul(pu[:, 2 * (h % 2) + c, :], left, ring[:, slot, 512 * c:512 * c + 512],
                                                    start=k == 0 and ring is ehi and left is hi,
                                                    stop=end and left is lo)
                    last.then_inc(ex_mm, 1)
                elif kind == "scatter":
                    scatter(8 * h + k // 2, k % 2, x, i * BODY_INNERS + (st.outer + 1), i * BODY_SCATTERS + st.scatter)
                elif kind == "slots":
                    pe.wait_ge(psu_lo, i * BODY_TURNS + (KT // 2 + st.turn + 1))
                    win = slice(32 * x, 32 * x + 128)
                    for t in (range(4) if h == 0 else (4,)):
                        last = nc.tensor.transpose(ps[:, st.turn % 2, 128 * (t % 4):128 * (t % 4) + 128],
                                                   oh[:, t, win], ident[:, :])
                    if h == 1:
                        for t in range(5):
                            last = nc.tensor.matmul(ps[:, st.turn % 2, 128:129], oh[:, t, win],
                                                    aff[:, t, ds(i * 4 + (2 * st.pair + x), 1)], start=t == 0, stop=t == 4)
                    last.then_inc(psu_mm, 1)
                elif kind == "gather":
                    gather(k, i * 2 + (st.pair + 2), st.turn % 2, i * BODY_TURNS + (KT // 2 + st.turn))
                elif kind == "turn":
                    pe.wait_ge(hid_done, i * BODY_INNERS + st.inner)
                    pe.wait_ge(psu_lo, i * BODY_TURNS + (KT // 2 + st.turn + 1))
                    for f in range(4):
                        last = nc.tensor.transpose(ps[:, st.turn % 2, 128 * f:128 * f + 128],
                                                   hid[:, 128 * f:128 * f + 128], ident[:, :])
                    last.then_inc(psu_mm, 1)
        for k in range(OLD_ITEMS, 2 * KT):
            scatter(k // 2, k % 2, 1, BODIES * BODY_INNERS + 2, BODIES * BODY_SCATTERS + k - OLD_ITEMS)
        pe.wait_ge(fin_sum, KT)
        mean_over_channels(hfin, ps, HALF, fin_mm)

    RV_LOGITS = 5
    RV_AFF = 5
    RV_MASK = RV_AFF + 2 + 2 * (CAPL // 8) + 2 * (CAPC // 8) + 1
    RV_MK5 = RV_MASK + 1
    RV_END = RV_MK5 + 1
    hfin, o_ = at("hfin", [128, N], F32, R0)
    fsq, o_ = at("fsq", [128, 2, N], F32, o_)
    f1, o_ = at("f1", [128, N], F32, o_)
    f2, o_ = at("f2", [128, N], F32, o_)
    f3, o_ = at("f3", [128, N], F32, o_)

    def scalar_program(act):
        def split_hi(slot, use, d, dk):
            act.wait_ge(raw_loaded[slot], 16 * (use + 1))
            act.wait_ge(dense_mm, d_done(d))
            nc.scalar.copy(whi[:, dk, :], raw[:, slot, :]).then_inc(hi_ready, 1)
            act.wait_ge(hi_ready, d + 1)
            act.sem_inc(raw_freed[slot], 1)

        def add_bias(n, bank):
            at_ = slice(n, n + 1) if isinstance(n, int) else ds(n, 1)
            return nc.scalar.activation(mod[:, at_, :].rearrange("p a c -> p (a c)"), bank[:, 128:130], ACT.Identity,
                                        bias=bada[:, at_])

        def ada_read_out(slot, use, n, bank, row):
            act.wait_ge(raw_freed[slot], 2 * use + 2)
            last = nc.scalar.copy(row, bank[0:2, 0:128])
            if n is not None:
                last = add_bias(n, bank)
            last.then_inc(ada_read, 1)

        act.sem_inc(ada_read, RAW)
        for freed in (att_exp, att_pt, att_out):
            act.sem_inc(freed, 1)
        act.wait_ge(small_loaded, 16 * 7)
        nc.scalar.activation(cond[:, :, :], cond[:, :, :], ACT.Silu).then_inc(cond_ready, 1)
        for kt in range(KT):
            act.wait_ge(x_loaded[kt // 4], 16)
            if kt >= 2:
                act.wait_ge(sq_summed, kt - 1)
            nc.scalar.activation((t2 if kt % 2 else t3)[:, :], xin[:, kt, :], ACT.Square).then_inc(sq_made, 1)
        for k in range(RAW):
            ada_read_out(*raw_use(0, 1, RAW, 0, k), None, pu[:, k, :], row4[0:2, k, :])
        act.wait_ge(norm_t, 2)
        nc.scalar.activation(rstd[:, :], t2[:, :], ACT.Sqrt).then_inc(norm_sq, 1)
        with act.Fori(1, A1 // RAW) as i:
            for k in range(RAW):
                ada_read_out(*raw_use(0, 1, RAW, i, k), i * RAW + (k - RAW), pu[:, k, :], row4[0:2, k, :])
        act.wait_ge(ada_read, RAW + A1)
        nc.scalar.copy(row1[0:2, :], row4[0:2, RAW - 1, :])
        act.wait_ge(ada_turned, 1)
        for k in range(RAW):
            last = add_bias(A1 - RAW + k, pu[:, k, :])
        last.then_inc(mod_ready, 1)
        act.wait_ge(gsc_ready, 1)
        for kt in range(KT):
            act.wait_ge(xn_ready, kt + 1)
            nc.scalar.activation(hhi[:, kt, 0:NL], xin[:, kt, 0:NL], ACT.Identity, scale=gsc[:, kt, 0:1],
                                 bias=mod[:, kt, 0:1])
            nc.scalar.activation(hhi[:, kt, NL:N], xin[:, kt, NL:N], ACT.Identity, scale=gsc[:, kt, 1:2],
                                 bias=mod[:, kt, 1:2]).then_inc(h_hi, 1)

        def ahead(i, k, body, first, stride, d0, count, nxt):
            if isinstance(i, int) and i * body + k + 2 >= count:
                if nxt is None:
                    return None
                m = i * body + k + 2 - count
                return (*raw_use(nxt, 1, U, 0, m), d0 + count + m)
            return (*raw_use(first, stride, body, i, k + 2), i * body + (d0 + k + 2))

        scalar_program.ahead = ahead
        act.wait_ge(h_lo, KT)
        for d in range(2):
            split_hi(*raw_use(G_Q, 1, U, 0, d), d, d % 2)
        for d in range(2 * NKV):
            if d < NKV:
                act.wait_ge(dense_mm, d + 1 + CREDIT)
                if d:
                    act.wait_ge(v_tr, d)
                    act.wait_ge(vx_stored, 16 * d)
                nc.scalar.copy(vst[:, :].rearrange("p (c n) -> p c n", c=2),
                               pu[:, 2 * (d % 2):2 * (d % 2) + 2, 0:HALF]).then_inc(v_read, 1)
                act.wait_ge(v_read, d + 1)
                act.sem_inc(psum_free[d % 2], 1)
            if 1 <= d <= NKV:
                n = d - 1
                act.wait_ge(v_tr, n + 1)
                if n:
                    act.wait_ge(v_stored, 16 * n)
                nc.scalar.copy(vtk[:, 0:640], pt[:, :, :].rearrange("p b n -> p (b n)")[:, 0:640]).then_inc(v_tok, 1)
            split_hi(*raw_use(G_Q, 1, U, 0, d + 2), d + 2, d % 2)
        with act.Fori(2 * NKV // U, QN // U) as i:
            for k in range(U):
                slot, use, d2 = ahead(i, k, U, G_Q, 1, 0, QN, G_G)
                split_hi(slot, use, d2, k % 2)

        def glu(i, k):
            n = i * U + k
            if k % 2 == 0:
                act.wait_ge(dense_mm, n + (QN + 1 + CREDIT))
                act.wait_ge(glu_z, i * (U // 2) + k // 2 + 1)
                nc.scalar.activation(gsig[:, :].rearrange("p (c n) -> p c n", c=2),
                                     pu[:, 2 * (k % 2):2 * (k % 2) + 2, 0:HALF], ACT.Sigmoid).then_inc(glu_sig, 1)
                act.wait_ge(glu_sig, i * (U // 2) + k // 2 + 1)
                act.sem_inc(psum_free[0], 1)
            got = ahead(i, k, U, G_G, 1, QN, GN, None)
            if got is None:
                m = i * U + k + 2 - GN
                slot, use = raw_use(G_S, 3, US, 0, m)
                got = (slot, use, QN + GN + m)
            split_hi(*got, k % 2)

        with act.Fori(0, GN // U - 1) as i:
            for k in range(U):
                glu(i, k)
        for k in range(U):
            glu(GN // U - 1, k)

        def softmax(i, n):
            h, j = STEPS[n]
            lo, hi = keys_of(j)
            w = 128 * (hi - lo)
            act.wait_ge(att_nm, i * NS + (n + 1))
            head = ds(i * GROUP + h, 1)
            if j < 4:
                nc.scalar.activation(pe_[:, 0:w], sm[:, 0:w], ACT.Exp, bias=nm[:, 0:1], scale=SCALE,
                                     accum_out=dn[:, 0:1])
                nc.scalar.activation(dn[:, 1:2], sinks[:, head], ACT.Exp, bias=nm[:, 0:1])
                nc.scalar.activation(pe_[:, w:w + PAST], ps[:, 1, 0:PAST], ACT.Exp, bias=nm[:, 0:1], scale=SCALE,
                                     accum_out=dn[:, 2:3]).then_inc(att_exp, 1)
            else:
                nc.scalar.activation(pe_[:, 0:NC], ps[:, 0, 0:NC], ACT.Exp, bias=nm[:, 0:1], scale=SCALE,
                                     accum_out=dn[:, 0:1])
                nc.scalar.activation(dn[:, 1:2], sinks[:, head], ACT.Exp, bias=nm[:, 0:1]).then_inc(att_exp, 1)

        def turned(i, n):
            h, j = STEPS[n]
            lo, hi = keys_of(j)
            w = 128 * (hi - lo + 2) if j < 4 else 128
            act.wait_ge(att_tr, i * NS + (n + 1) + 1)
            last = nc.scalar.copy(pt_sb[:, 0:min(w, 512)], pt[:, 0, 0:min(w, 512)])
            if w > 512:
                last = nc.scalar.copy(pt_sb[:, 512:w], ps[:, 1, 0:w - 512])
            last.then_inc(att_pt, 1)

        def head_out(i, n):
            act.wait_ge(att_pv, i * NS + (n + 2))
            if n >= 2:
                act.wait_ge(att_stored[n % 2], (i * (NS // 2) + n // 2) * 16)
            nc.scalar.copy(ao[:, n % 2, :], pt[:, 0, 0:128]).then_inc(att_out, 1)

        def stage_s(i):
            def next_unit(k):
                slot, use, d2 = ahead(i, k, US, G_S, 3, QN + GN, SN, G_T)
                split_hi(slot, use, d2, k % 2)

            for k in range(US):
                steps = list(range(CUT[k], CUT[k + 1]))
                for x, n in enumerate(steps):
                    softmax(i, n)
                    if x == 0 and k:
                        next_unit(k - 1)
                    turned(i, n)
                    if x < 2:
                        at_ = G_S + 3 * k + 1 + x
                        ada_read_out(at_ % RAW, at_ // RAW + i * (3 * US // RAW), i * (2 * US) + (A1 + 2 * k + x - 1),
                                     pt[:, 1, :], row1[0:2, :])
                    head_out(i, n)
                act.wait_ge(dense_mm, i * US + (QN + GN + k + 1 + CREDIT))
                if k >= 2:
                    act.wait_ge(th_stored[k % 2], (i * (US // 2) + k // 2) * 16)
                nc.scalar.activation(th[:, k % 2, :].rearrange("p (c n) -> p c n", c=2),
                                     pu[:, 2 * (k % 2):2 * (k % 2) + 2, 0:HALF], ACT.Tanh,
                                     scale=0.5).then_inc(th_ready, 1)
                act.wait_ge(th_ready, i * US + (k + 1))
                act.sem_inc(psum_free[k % 2], 1)
            next_unit(US - 1)
            for b in range(2):
                act.wait_ge(att_stored[b], (i * (NS // 2) + NS // 2) * 16)
                act.wait_ge(th_stored[b], (i * (US // 2) + US // 2) * 16)

        with act.Fori(0, SN // US - 1) as i:
            stage_s(i)
        stage_s(SN // US - 1)
        act.wait_ge(ada_turned, 2)
        add_bias(ADA - 1, pt[:, 1, :]).then_inc(mod_ready, 1)

        D_T = QN + GN + SN
        act.wait_ge(dense_mm, D_T + CREDIT)
        for m in range(KT):
            act.wait_ge(attn_loaded[m % 4], 16 * (m // 4 + 1))
            nc.scalar.copy(hhi[:, m, :], att4[:, m % 4, :]).then_inc(attn_hi, 1)

        def ln_squares():
            for m in range(CT):
                act.wait_ge(ln_c, 1 + m + 1)
                if m >= 2:
                    act.wait_ge(ln_sum2, m - 1)
                nc.scalar.activation(lq[:, m % 2, 0:CO], zt[:, m, 0:CO], ACT.Square).then_inc(ln_sq, 1)

        def ln_root():
            act.wait_ge(ln_c, LN_R)
            nc.scalar.activation(ls2[:, 0:CO], ls3[:, 0:CO], ACT.Sqrt).then_inc(norm_sq, 1)

        def ln_swish():
            act.wait_ge(ln_c, LN_RSTD)
            for m in range(CT):
                act.wait_ge(ln_c, LN_RSTD + m + 1)
                if m >= 2:
                    act.wait_ge(ln_lo, m - 1)
                row = lt2 if m % 2 else lt1
                for c0, z0, w in ((0, 0, NL), (NL, NL + 2 * PAD, NC)):
                    last = nc.scalar.activation(row[:, c0:c0 + w], zt[:, m, z0:z0 + w], ACT.Silu,
                                                scale=convp[:, 1, m:m + 1], bias=convp[:, 2, m:m + 1])
                last.then_inc(ln_act, 1)
                act.wait_ge(ln_act, m + 1)
                if m == 0:
                    act.wait_ge(ln_c, LN_RSTD + CT)
                nc.scalar.copy(ahi[:, m, :], row[:, 0:N]).then_inc(ln_hi, 1)

        def finish_split(t, base_d, first, n_next, n):
            if t + 2 < n:
                split_hi(*raw_use(first, 1, U, 0, t + 2), base_d + t + 2, t % 2)
            elif n_next is not None:
                split_hi(*raw_use(n_next, 1, U, 0, t + 2 - n), base_d + t + 2, t % 2)

        for t in range(TN):
            act.wait_ge(dense_mm, D_T + t + 1 + CREDIT)
            finish_split(t, D_T, G_T, G_C, TN)
            if t == 1:
                ln_squares()
            if t == 3:
                ln_root()
            if t == 4:
                ln_swish()
        for m in range(KT):
            act.wait_ge(mix_sum, m + 1)
            nc.scalar.copy(hhi[:, m, :], (lt2 if m % 2 else lt1)[:, 0:N]).then_inc(mix_hi, 1)
            if m % 2:
                c = m // 2
                finish_split(c, D_T + TN, G_C, G_O, CN)
        for t in range(ON):
            act.wait_ge(res_done, t + 1)
            if t:
                act.wait_ge(res_sum, t)
            nc.scalar.activation(sq[:, :], xr[:, t, :], ACT.Square).then_inc(res_sq, 1)
            finish_split(t, D_T + TN + CN, G_O, None, ON)
        act.wait_ge(norm_t, 4 + 4)
        nc.scalar.activation(e1[:, :], e3[:, :], ACT.Sqrt).then_inc(norm_sq, 1)
        for kt in range(KT):
            act.wait_ge(h2_vec, kt + 1)
            if kt:
                act.wait_ge(h2_tr, kt)
            row = (e2 if kt % 2 else e3)
            nc.scalar.activation(h2t[:, 0, 0:NL], row[:, 0:NL], ACT.Identity, scale=gsc[:, kt, 0:1],
                                 bias=mod[:, 3 * KT + kt, 0:1])
            nc.scalar.activation(h2t[:, 0, NL:N], row[:, NL:N], ACT.Identity, scale=gsc[:, kt, 1:2],
                                 bias=mod[:, 3 * KT + kt, 1:2]).then_inc(h2_act, 1)
            if kt >= 1:
                turned_hi(kt - 1)
        turned_hi(KT - 1)
        act.wait_ge(h2_tr, KT)
        nc.scalar.activation(lgT[:, :], ps[0:16, :, :].rearrange("p b n -> p (b n)")[:, 0:N], ACT.Identity,
                             bias=brt[:, 0:1]).then_inc(rt_act, 1)
        act.wait_ge(rt_vec, 2)
        nc.scalar.activation(sm5[:, :, :], sm5[:, :, :], ACT.Exp).then_inc(rt_act, 1)

        act.wait_ge(rt_vec, RV_END)

        def piece_hi(i, slot):
            unit, use = raw_use(G_E, 1, BODY_PIECES // 2, i, slot // 2)
            act.wait_ge(raw_loaded[unit], 16 * (use + 1))
            cols = slice(1024 * (slot % 2), 1024 * (slot % 2) + 1024)
            nc.scalar.copy(ehi[:, slot % 3, :], raw[:, unit, cols]).then_inc(ex_hi, 1)

        def gather_hi(g, buf, bank, u):
            act.wait_ge(psu_mm, u + 1)
            v = ps[:, bank, 0:2 * SLOTS].rearrange("p (k s) -> p k s", k=2)
            nc.scalar.copy(xhi[:, buf, 2 * g:2 * g + 2, :], v).then_inc(psu_hi, 1)

        def outer_hi(x, h, pieces, scattered, turned):
            act.wait_ge(ex_mm, pieces)
            act.wait_ge(sc_mm, scattered)
            act.wait_ge(psu_lo, turned + 2)
            nc.scalar.activation(yhi[:, :].rearrange("p (c n) -> p c n", c=2), pu[:, 2 * h:2 * h + 2, :],
                                 ACT.Identity, scale=gates[:, x:x + 1]).then_inc(y_hi, 1)

        for n in range(AHEAD):
            piece_hi(0, n)
        for g in range(KT // 2):
            gather_hi(g, 0, g % 2, g)

        def experts(i, last_body):
            for st in body_steps():
                kind, x, h, k = st.what
                if kind == "piece":
                    if not (last_body and st.piece + AHEAD >= BODY_PIECES):
                        act.wait_ge(ex_mm, i * BODY_PIECES + (st.piece + 1))
                        piece_hi(i, st.piece + AHEAD)
                elif kind == "slots":
                    act.wait_ge(psu_mm, i * BODY_TURNS + (KT // 2 + st.turn + 1))
                    if h == 0:
                        nc.scalar.copy(oht[:, x, 0:256], ps[:, st.turn % 2, 0:256]).then_inc(psu_hi, 1)
                    else:
                        nc.scalar.copy(oht[:, x, NL:N], ps[:, st.turn % 2, 0:NC]).then_inc(psu_hi, 1)
                elif kind == "gather":
                    gather_hi(k, (st.pair + 1) % 2, st.turn % 2, i * BODY_TURNS + (KT // 2 + st.turn))
                elif kind == "turn":
                    act.wait_ge(psu_mm, i * BODY_TURNS + (KT // 2 + st.turn + 1))
                    nc.scalar.copy(hthi[:, 4 * h:4 * h + 4, :],
                                   ps[:, st.turn % 2, :].rearrange("p (f s) -> p f s", f=4)).then_inc(psu_hi, 1)
                elif kind == "inner":
                    act.wait_ge(ex_mm, i * BODY_PIECES + st.piece)
                    nc.scalar.activation(hid[:, :], pu[:, 2 * h, :], ACT.Silu).then_inc(hid_silu, 1)
                elif kind == "outer":
                    outer_hi(x, h, i * BODY_PIECES + st.piece, i * BODY_SCATTERS + st.scatter,
                             i * BODY_TURNS + (KT // 2 + st.slots_done))

        with act.Fori(0, BODIES - 1) as i:
            experts(i, False)
        experts(BODIES - 1, True)
        outer_hi(1, 1, BODIES * BODY_PIECES, BODIES * BODY_SCATTERS + KT - OLD_ITEMS, BODIES * BODY_TURNS)
        for kt in range(KT):
            act.wait_ge(sc_add, 2 + BODIES * BODY_SCATTERS - OLD_ITEMS + 2 * kt + 2)
            if kt >= 2:
                act.wait_ge(fin_sum, kt - 1)
            nc.scalar.activation(fsq[:, kt % 2, :], xr[:, kt, :], ACT.Square).then_inc(fin_sq, 1)
        act.wait_ge(fin_c, 2)
        nc.scalar.activation(f1[:, :], f3[:, :], ACT.Sqrt).then_inc(norm_sq, 1)

    def d_done(d):
        D_C = QN + GN + SN + TN
        if isinstance(d, int):
            prev = d - SPL
            if prev < D_C:
                return prev + 1 + CREDIT
            if prev < D_C + CN:
                return D_C + 2 * (prev - D_C + 1) + CREDIT
            return prev + CN + 1 + CREDIT
        return d + (1 + CREDIT - SPL)

    LN_R = 1 + CT + 2
    LN_RSTD = LN_R + 4
    ln_sum2 = sem("ln_sum2")

    def turned_hi(kt):
        nc.scalar.wait_ge(h2_tr, kt + 1)
        nc.scalar.copy(h2[:, :, kt * 128:kt * 128 + 128],
                       pu[:, 2 * (kt % 2):2 * (kt % 2) + 2, :].rearrange("p b n -> p (b n)")[:, 0:640]
                       .rearrange("p (t c) -> p t c", c=128)).then_inc(h2_hi, 1)

    def vector_program(vec):
        chain = [0]

        def link(ins):
            chain[0] += 1
            ins.then_inc(vec_done, 1)
            vec.wait_ge(vec_done, chain[0])

        def split_lo(slot, use, d, dk):
            vec.wait_ge(hi_ready, d + 1)
            nc.vector.tensor_tensor(wlo[:, dk, :], raw[:, slot, :], whi[:, dk, :].bitcast(F32),
                                    ALU.subtract).then_inc(lo_ready, 1)
            vec.wait_ge(lo_ready, d + 1)
            vec.sem_inc(raw_freed[slot], 1)

        ahead = scalar_program.ahead
        for b in range(2):
            vec.sem_inc(psum_free[b], 1)
        for used in (glu_z, rope_out, conv_done):
            vec.sem_inc(used, 1)
        nc.vector.memset(t1[:, :], 0.0).then_inc(norm_t, 1)
        for kt in range(KT):
            vec.wait_ge(sq_made, kt + 1)
            if kt == 0:
                vec.wait_ge(norm_t, 1)
            else:
                vec.wait_ge(sq_summed, kt)
            nc.vector.tensor_tensor(t1[:, :], t1[:, :], (t2 if kt % 2 else t3)[:, :], ALU.add).then_inc(sq_summed, 1)
        vec.wait_ge(norm_mm, 1)
        c2 = "p (c n) -> p c n"
        link(nc.vector.tensor_scalar(t4[:, :].rearrange(c2, c=2), ps[:, :, 0:HALF], EPS, None, ALU.add))
        nc.vector.reciprocal(t2[:, :], t4[:, :]).then_inc(norm_t, 1)
        vec.wait_ge(norm_sq, 1)
        link(nc.vector.tensor_tensor(t3[:, :], rstd[:, :], rstd[:, :], ALU.mult))
        link(nc.vector.tensor_tensor(t3[:, :], t3[:, :], t4[:, :], ALU.mult))
        link(nc.vector.tensor_scalar(t3[:, :], t3[:, :], -0.5, 1.5, ALU.mult, ALU.add))
        link(nc.vector.tensor_tensor(rstd[:, :], rstd[:, :], t3[:, :], ALU.mult))
        for kt in range(KT):
            nc.vector.tensor_tensor(xin[:, kt, :], xin[:, kt, :], rstd[:, :], ALU.mult).then_inc(xn_ready, 1)
        vec.wait_ge(mod_ready, 1)
        vec.wait_ge(small_loaded, 16 * 7)
        nc.vector.tensor_scalar(negsink[:, :], sinks[:, :], -1.0, None, ALU.mult)
        nc.vector.scalar_tensor_tensor(out=gsc[:, :, :], in0=mod[:, KT:2 * KT, :], scalar=1.0,
                                       in1=norms[:, 0, :, :], op0=ALU.add, op1=ALU.mult).then_inc(gsc_ready, 1)
        vec.wait_ge(gsc_ready, 1)
        for kt in range(KT):
            vec.wait_ge(h_hi, kt + 1)
            vec.wait_ge(xn_ready, kt + 1)
            nc.vector.tensor_scalar(xin[:, kt, 0:NL], xin[:, kt, 0:NL], gsc[:, kt, 0:1], mod[:, kt, 0:1],
                                    ALU.mult, ALU.add)
            link(nc.vector.tensor_scalar(xin[:, kt, NL:N], xin[:, kt, NL:N], gsc[:, kt, 1:2], mod[:, kt, 1:2],
                                         ALU.mult, ALU.add))
            nc.vector.tensor_tensor(hlo[:, kt, :], xin[:, kt, :], hhi[:, kt, :].bitcast(F32),
                                    ALU.subtract).then_inc(h_lo, 1)
        for d in range(2):
            split_lo(*raw_use(G_Q, 1, U, 0, d), d, d % 2)

        def rotate(i, d, k, n):
            vec.wait_ge(dense_mm, d + (1 + CREDIT))
            src = pu[:, 2 * (k % 2):2 * (k % 2) + 2, 0:HALF]
            vec.wait_ge(rope_out, n + 1)
            nc.vector.tensor_tensor(ra[:, :].rearrange(c2, c=2), src, cost[:, :].rearrange(c2, c=2),
                                    ALU.mult).then_inc(rope_a, 1)
            nc.vector.tensor_tensor(rb[:, :].rearrange(c2, c=2), src, sint[:, :].rearrange(c2, c=2),
                                    ALU.mult).then_inc(rope_b, 1)
            vec.wait_ge(rope_b, n + 1)
            vec.sem_inc(psum_free[k % 2], 1)
            vec.wait_ge(rope_swapped, n * 64 + 64)
            if i is None:
                stored = 32 * n
            else:
                stored = n * 16 + 16 * NKV
            vec.wait_ge(rope_stored, stored)
            nc.vector.tensor_tensor(ro[:, :], ra[:, :], rbs[:, :], ALU.add).then_inc(rope_out, 1)

        for d in range(2 * NKV):
            if d >= NKV:
                if d == NKV:
                    vec.wait_ge(tabs_loaded, 48)
                rotate(None, d, d % 2, d - NKV)
            split_lo(*raw_use(G_Q, 1, U, 0, d + 2), d + 2, d % 2)
        with vec.Fori(2 * NKV // U, QN // U) as i:
            for k in range(U):
                rotate(i, i * U + k, k, i * U + (k - NKV))
                slot, use, d2 = ahead(i, k, U, G_Q, 1, 0, QN, G_G)
                split_lo(slot, use, d2, k % 2)
        vec.wait_ge(rope_stored, 16 * (2 * NKV + NH))
        vec.wait_ge(v_stored, 16 * NKV)
        vec.wait_ge(vx_stored, 16 * NKV)
        nc.vector.memset(zt[:, :, 0:PAD], 0.0)
        nc.vector.memset(zt[:, :, PAD + NL:PAD + NL + 2 * PAD], 0.0)
        nc.vector.memset(zt[:, :, ZW - PAD:ZW], 0.0).then_inc(z_zero, 1)
        ztf = zt[:, :, :].rearrange("p m c -> p (m c)")

        def glu(i, k):
            if k % 2 == 1:
                vec.wait_ge(dense_mm, i * U + (QN + k + 1 + CREDIT))
                vec.wait_ge(glu_sig, i * (U // 2) + (k // 2 + 1))
                for t, c, c0, c1 in SEGS:
                    z0 = i * (U // 2 * ZW) + (k // 2 * ZW + PAD + t + (2 * PAD if t >= NL else 0))
                    last = nc.vector.tensor_tensor(ztf[:, ds(z0, c1 - c0)], pu[:, 2 + c, c0:c1],
                                                   gsig[:, t:t + c1 - c0], ALU.mult)
                last.then_inc(glu_z, 1)
                vec.wait_ge(glu_z, i * (U // 2) + (k // 2 + 1) + 1)
                vec.sem_inc(psum_free[1], 1)
            got = ahead(i, k, U, G_G, 1, QN, GN, None)
            if got is None:
                m = i * U + k + 2 - GN
                got = (*raw_use(G_S, 3, US, 0, m), QN + GN + m)
            split_lo(*got, k % 2)

        with vec.Fori(0, GN // U - 1) as i:
            for k in range(U):
                glu(i, k)
        for k in range(U):
            glu(GN // U - 1, k)

        def maxima(i, n):
            h, j = STEPS[n]
            lo, hi = keys_of(j)
            w = 128 * (hi - lo)
            s = i * NS + n
            vec.wait_ge(att_qk, s + 11)
            v = i * (4 * NS) + 4 * n
            if j < 4:
                nc.vector.reduce_max(mx[:, 0:1], ps[:, 1, 0:PAST], AX).then_inc(att_v, 1)
                vec.wait_ge(att_v, v + 1)
                vec.sem_inc(vec_passed, 1)
                m0 = 128 if j == 0 else 0
                nc.vector.tensor_tensor_reduce(out=sm[:, 0:w], in0=ps[:, 0, 0:w], in1=mask[:, m0:m0 + w], scale=1.0,
                                               scalar=mx[:, 0:1], op0=ALU.add, op1=ALU.max,
                                               accum_out=mx[:, 1:2]).then_inc(att_v, 1)
            else:
                nc.vector.reduce_max(mx[:, 1:2], ps[:, 0, 0:NC], AX).then_inc(att_v, 2)
            vec.wait_ge(att_v, v + 2)
            nc.vector.tensor_scalar(nm[:, 0:1], mx[:, 1:2], -SCALE, negsink[:, ds(i * GROUP + h, 1)], ALU.mult,
                                    ALU.min).then_inc(att_nm, 1)

        def normalise(i, n):
            h, j = STEPS[n]
            lo, hi = keys_of(j)
            w = 128 * (hi - lo) + PAST if j < 4 else NC
            v = i * (4 * NS) + 4 * n
            vec.wait_ge(att_exp, i * NS + (n + 1) + 1)
            nc.vector.reduce_sum(rd[:, 0:1], dn[:, 0:3 if j < 4 else 2], AX).then_inc(att_v, 1)
            vec.wait_ge(att_v, v + 3)
            nc.vector.reciprocal(rd[:, 1:2], rd[:, 0:1]).then_inc(att_v, 1)
            vec.wait_ge(att_v, v + 4)
            vec.wait_ge(att_tr, i * NS + n + 1)
            nc.vector.tensor_scalar(pn[:, 0:w], pe_[:, 0:w], rd[:, 1:2], None, ALU.mult).then_inc(att_pn, 1)

        def conv(i, k, part, parts):
            m_off = k // 4
            lo_ = (k % 4) * 8
            taps_ = list(range(lo_, min(lo_ + 8, TAPS)))
            a0, a1 = len(taps_) * part // parts, len(taps_) * (part + 1) // parts
            for x in taps_[a0:a1]:
                tap = TAPS - 1 - x
                done = i * (2 * TAPS) + (m_off * TAPS + x)
                zb = i * (2 * ZW) + (m_off * ZW + tap)
                w = taps[:, :, :].rearrange("p m t -> p (m t)")[:, ds(i * (2 * TAPS) + (m_off * TAPS + tap), 1)]
                vec.wait_ge(conv_done, done + 1)
                if x == 0:
                    nc.vector.tensor_scalar(ctmp[:, :], ztf[:, ds(zb, CO)], w, convp[:, 0, ds(i * 2 + m_off, 1)],
                                            ALU.mult, ALU.add).then_inc(conv_done, 1)
                else:
                    dst = ctmp[:, :] if tap else ztf[:, ds(zb, CO)]
                    nc.vector.scalar_tensor_tensor(out=dst, in0=ztf[:, ds(zb, CO)], scalar=w, in1=ctmp[:, :],
                                                   op0=ALU.mult, op1=ALU.add).then_inc(conv_done, 1)

        vec.wait_ge(z_zero, 1)
        vec.wait_ge(tabs_loaded, 48)

        def stage_s(i):
            def next_unit(k):
                slot, use, d2 = ahead(i, k, US, G_S, 3, QN + GN, SN, G_T)
                split_lo(slot, use, d2, k % 2)

            for k in range(US):
                steps = list(range(CUT[k], CUT[k + 1]))
                for x, n in enumerate(steps):
                    maxima(i, n)
                    normalise(i, n)
                    if x == 0 and k:
                        next_unit(k - 1)
                    conv(i, k, x, len(steps))
            next_unit(US - 1)

        with vec.Fori(0, SN // US - 1) as i:
            stage_s(i)
        stage_s(SN // US - 1)

        D_T = QN + GN + SN
        vec.wait_ge(mod_ready, 2)
        nc.vector.tensor_scalar(ghalf[:, :, :], mod[:, 2 * KT:3 * KT, :], 0.5, None, ALU.mult)
        link(nc.vector.scalar_tensor_tensor(out=gsc[:, :, :], in0=mod[:, 4 * KT:5 * KT, :], scalar=1.0,
                                            in1=norms[:, 1, :, :], op0=ALU.add, op1=ALU.mult))
        for m in range(KT):
            vec.wait_ge(attn_hi, m + 1)
            nc.vector.tensor_tensor(hlo[:, m, :], att4[:, m % 4, :], hhi[:, m, :].bitcast(F32),
                                    ALU.subtract).then_inc(attn_lo, 1)

        def finish_split(t, base_d, first, n_next, n):
            if t + 2 < n:
                split_lo(*raw_use(first, 1, U, 0, t + 2), base_d + t + 2, t % 2)
            elif n_next is not None:
                split_lo(*raw_use(n_next, 1, U, 0, t + 2 - n), base_d + t + 2, t % 2)

        lnc = [0]

        def ln(ins):
            lnc[0] += 1
            ins.then_inc(ln_c, 1)

        def ln_link(ins):
            ln(ins)
            vec.wait_ge(ln_c, lnc[0])

        def ln_mean():
            vec.wait_ge(conv_done, TAPS * CT + 1)
            nc.vector.tensor_reduce(ls1[:, 0:CO], zt[:, :, 0:CO].rearrange("p m c -> p c m"), AX,
                                    ALU.add).then_inc(ln_sum, 1)

        def ln_centre():
            vec.wait_ge(ln_mm, 1)
            ln_link(nc.vector.tensor_scalar(ls2[:, 0:CO].rearrange(c2, c=2), ps[:, :, 0:CO // 2], D / CW, None,
                                            ALU.mult))
            for m in range(CT):
                ln(nc.vector.tensor_tensor(zt[:, m, 0:CO], zt[:, m, 0:CO], ls2[:, 0:CO], ALU.subtract))
            for m in range(CT):
                vec.wait_ge(ln_sq, m + 1)
                row = lq[:, m % 2, 0:CO]
                if m == 0:
                    nc.vector.tensor_copy(ls1[:, 0:CO], row).then_inc(ln_sum2, 1)
                else:
                    vec.wait_ge(ln_sum2, m)
                    nc.vector.tensor_tensor(ls1[:, 0:CO], ls1[:, 0:CO], row, ALU.add).then_inc(
                        ln_sum2 if m < CT - 1 else ln_sum, 1)

        def ln_rstd():
            vec.wait_ge(ln_mm, 2)
            ln_link(nc.vector.tensor_scalar(ls1[:, 0:CO].rearrange(c2, c=2), pt[:, :, 0:CO // 2], D / CW, EPS,
                                            ALU.mult, ALU.add))
            ln_link(nc.vector.reciprocal(ls3[:, 0:CO], ls1[:, 0:CO]))
            assert lnc[0] == LN_R, lnc
            vec.wait_ge(norm_sq, 2)
            ln_link(nc.vector.tensor_tensor(ls3[:, 0:CO], ls2[:, 0:CO], ls2[:, 0:CO], ALU.mult))
            ln_link(nc.vector.tensor_tensor(ls3[:, 0:CO], ls3[:, 0:CO], ls1[:, 0:CO], ALU.mult))
            ln_link(nc.vector.tensor_scalar(ls3[:, 0:CO], ls3[:, 0:CO], -0.5, 1.5, ALU.mult, ALU.add))
            ln_link(nc.vector.tensor_tensor(ls2[:, 0:CO], ls2[:, 0:CO], ls3[:, 0:CO], ALU.mult))
            assert lnc[0] == LN_RSTD, lnc
            for m in range(CT):
                ln(nc.vector.tensor_tensor(zt[:, m, 0:CO], zt[:, m, 0:CO], ls2[:, 0:CO], ALU.mult))

        def ln_low():
            for m in range(CT):
                vec.wait_ge(ln_hi, m + 1)
                row = lt2 if m % 2 else lt1
                nc.vector.tensor_tensor(alo[:, m, :], row[:, 0:N], ahi[:, m, :].bitcast(F32),
                                        ALU.subtract).then_inc(ln_lo, 1)

        vec.wait_ge(attn_lo, KT)
        for t in range(TN):
            vec.wait_ge(dense_mm, D_T + t + 1 + CREDIT)
            vec.wait_ge(gl_loaded[t % 2], 16 * (t // 2 + 1))
            if t >= 2:
                vec.wait_ge(mo_stored[t % 2], 16 * (t // 2))
            nc.vector.scalar_tensor_tensor(out=mo[:, t % 2, :].rearrange(c2, c=2),
                                           in0=gl[:, t % 2, :].rearrange(c2, c=2), scalar=1.0,
                                           in1=pu[:, 2 * (t % 2):2 * (t % 2) + 2, 0:HALF], op0=ALU.add,
                                           op1=ALU.mult).then_inc(mo_ready, 1)
            vec.wait_ge(mo_ready, t + 1)
            vec.sem_inc(psum_free[t % 2], 1)
            finish_split(t, D_T, G_T, G_C, TN)
            if t == 0:
                ln_mean()
            if t == 1:
                ln_centre()
            if t == 3:
                ln_rstd()
            if t == 4:
                ln_low()
        for m in range(KT):
            p = D_T + TN + m
            vec.wait_ge(dense_mm, p + 1 + CREDIT)
            use = KT // 2 + m // 2 + 1
            vec.wait_ge(gl_loaded[m % 2], 16 * use)
            vec.wait_ge(ml_loaded[m % 2], 16 * (m // 2 + 1))
            row = (lt2 if m % 2 else lt1)[:, 0:N]
            if m >= 2:
                vec.wait_ge(mix_hi, m - 1)
            link(nc.vector.scalar_tensor_tensor(out=row.rearrange(c2, c=2), in0=gl[:, m % 2, :].rearrange(c2, c=2),
                                                scalar=1.0, in1=pu[:, 2 * (m % 2):2 * (m % 2) + 2, 0:HALF],
                                                op0=ALU.add, op1=ALU.mult))
            vec.sem_inc(psum_free[m % 2], 1)
            nc.vector.tensor_tensor(row, row, mo[:, m % 2, :], ALU.add).then_inc(mix_sum, 1)
            vec.wait_ge(mix_hi, m + 1)
            nc.vector.tensor_tensor(hlo[:, m, :], row, hhi[:, m, :].bitcast(F32), ALU.subtract).then_inc(mix_lo, 1)
            if m % 2:
                finish_split(m // 2, D_T + TN, G_C, G_O, CN)
        link(nc.vector.memset(ssum[:, :], 0.0))
        vec.wait_ge(xr_loaded, 64)
        for t in range(ON):
            p = D_T + TN + 2 * CN + t
            vec.wait_ge(dense_mm, p + 1 + CREDIT)
            for t0, c, c0, c1 in SEGS:
                s = 1 if t0 >= NL else 0
                last = nc.vector.scalar_tensor_tensor(out=xr[:, t, t0:t0 + c1 - c0],
                                                      in0=pu[:, 2 * (t % 2) + c, c0:c1],
                                                      scalar=ghalf[:, t, s:s + 1], in1=xr[:, t, t0:t0 + c1 - c0],
                                                      op0=ALU.mult, op1=ALU.add)
            last.then_inc(res_done, 1)
            vec.wait_ge(res_done, t + 1)
            vec.sem_inc(psum_free[t % 2], 1)
            finish_split(t, D_T + TN + CN, G_O, None, ON)
            vec.wait_ge(res_sq, t + 1)
            if t:
                vec.wait_ge(res_sum, t)
            nc.vector.tensor_tensor(ssum[:, :], ssum[:, :], sq[:, :], ALU.add).then_inc(res_sum, 1)
        nt = [2]

        def ntl(ins):
            nt[0] += 1
            ins.then_inc(norm_t, 1)
            vec.wait_ge(norm_t, nt[0])

        vec.wait_ge(norm_mm, 2)
        ntl(nc.vector.memset(posm[:, :, :], 0.0))
        ntl(nc.vector.memset(aff[:, :, :], 0.0))
        ntl(nc.vector.memset(top8[:, :], 0.0))
        ntl(nc.vector.memset(mk5[:, :, :], 0.0))
        ntl(nc.vector.tensor_scalar(e2[:, :].rearrange(c2, c=2), ps[:, :, 0:HALF], EPS, None, ALU.add))
        ntl(nc.vector.reciprocal(e3[:, :], e2[:, :]))
        vec.wait_ge(norm_sq, 3)
        ntl(nc.vector.tensor_tensor(e3[:, :], e1[:, :], e1[:, :], ALU.mult))
        ntl(nc.vector.tensor_tensor(e3[:, :], e3[:, :], e2[:, :], ALU.mult))
        ntl(nc.vector.tensor_scalar(e3[:, :], e3[:, :], -0.5, 1.5, ALU.mult, ALU.add))
        ntl(nc.vector.tensor_tensor(e1[:, :], e1[:, :], e3[:, :], ALU.mult))

        for kt in range(KT):
            if kt >= 2:
                vec.wait_ge(h2_act, kt - 1)
            nc.vector.tensor_tensor((e2 if kt % 2 else e3)[:, :], xr[:, kt, :], e1[:, :], ALU.mult).then_inc(h2_vec, 1)

        rv = [0]

        def rt(ins):
            rv[0] += 1
            ins.then_inc(rt_vec, 1)
            vec.wait_ge(rt_vec, rv[0])

        vec.wait_ge(rt_pe, 1)
        lg = pt[:, 0, 0:5 * NE].rearrange("p (t e) -> p t e", e=NE)
        rt(nc.vector.tensor_reduce(sm5b[:, :], lg, AX, ALU.max))
        rt(nc.vector.tensor_tensor(sm5[:, :, :], lg, sm5b[:, :].unsqueeze(2).to_broadcast([128, 5, NE]),
                                   ALU.subtract))
        vec.wait_ge(rt_act, 2)
        rt(nc.vector.tensor_reduce(sm5b[:, :], sm5[:, :, :], AX, ALU.add))
        rt(nc.vector.reciprocal(sm5b[:, :], sm5b[:, :]))
        rt(nc.vector.tensor_tensor(aff[:, :, 0:NE], sm5[:, :, :], sm5b[:, :].unsqueeze(2).to_broadcast([128, 5, NE]),
                                   ALU.mult))
        assert rv[0] == RV_AFF
        vec.wait_ge(rt_pe, 2)
        rt(nc.vector.tensor_copy(affT[:, :], ps[0:16, :, :].rearrange("p b n -> p (b n)")[:, 0:N]))
        rt(nc.vector.tensor_copy(work[:, :], affT[:, :]))
        for t0, t1_, cap in ((0, NL, CAPL), (NL, N, CAPC)):
            for r in range(cap // 8):
                rt(nc.vector.max(top8[:, :], work[:, t0:t1_]))
                rt(nc.vector.match_replace(work[:, t0:t1_], top8[:, :], work[:, t0:t1_], -1.0))
        rt(nc.vector.tensor_scalar(work[:, :], work[:, :], 0.0, None, ALU.is_lt))
        assert rv[0] == RV_MASK, (rv, RV_MASK)
        vec.wait_ge(rt_pe, 3)
        rt(nc.vector.tensor_copy(mk5[:, :, :], pt[:, 0, 0:5 * NE].rearrange("p (t e) -> p t e", e=NE)))
        assert rv[0] == RV_MK5
        vec.wait_ge(rt_pe, 4)
        rt(nc.vector.tensor_tensor(posm[:, :, 0:NE], pt[:, 1, 0:5 * NE].rearrange("p (t e) -> p t e", e=NE),
                                   mk5[:, :, :], ALU.mult))
        vec.wait_ge(rt_loaded, 64)

        assert rv[0] == RV_END, (rv, RV_END)

        zeroed = sem("slots_zeroed")
        nc.vector.memset(oh[:, :, :], 0.0).then_inc(zeroed, 1)
        nc.vector.memset(zeros[:, :], 0.0).then_inc(zeroed, 1)
        vec.wait_ge(zeroed, 2)
        nc.vector.tensor_copy(yhi[:, :], zeros[:, :]).then_inc(zeroed, 1)
        nc.vector.tensor_copy(ylo[:, :], zeros[:, :]).then_inc(zeroed, 1)
        nc.vector.tensor_copy(oht[:, 1, :], zeros[:, 0:N]).then_inc(zeroed, 1)
        nc.vector.memset(gates[:, :], 0.0).then_inc(zeroed, 1)
        nc.vector.memset(pu[:, 2:4, :], 0.0).then_inc(zeroed, 1)
        vec.wait_ge(zeroed, 7)
        vec.sem_inc(psu_lo, 2)
        vec.sem_inc(sc_add, 2)
        vec.sem_inc(y_lo, 1)

        def select(pair):
            b4 = [128, 4, CAPL]
            for x in range(2):
                e = pair * 2 + x
                at_ = ds(e, 1) if not isinstance(e, int) else slice(e, e + 1)
                lat, ctx = LAT0[x], CTX0[x]
                nc.vector.tensor_tensor(oh[:, 0:4, lat:lat + CAPL], posm[:, 0:4, at_].to_broadcast(b4),
                                        iota[:, 0:CAPL].unsqueeze(1).to_broadcast(b4), ALU.is_equal)
                last = nc.vector.tensor_tensor(oh[:, 4, ctx:ctx + CAPC], posm[:, 4, at_].to_broadcast([128, CAPC]),
                                               iota[:, 0:CAPC], ALU.is_equal)
            last.then_inc(sel_made, 1)

        def piece_lo(n, slot):
            vec.wait_ge(ex_hi, n + 1)
            cols = slice(1024 * (slot % 2), 1024 * (slot % 2) + 1024)
            unit = (G_E + slot // 2) % RAW
            nc.vector.tensor_tensor(elo[:, slot % 3, :], raw[:, unit, cols], ehi[:, slot % 3, :].bitcast(F32),
                                    ALU.subtract).then_inc(ex_lo, 1)
            if slot % 2:
                vec.wait_ge(ex_lo, n + 1)
                vec.sem_inc(raw_freed[unit], 2)

        def gather_lo(g, buf, bank, u):
            vec.wait_ge(psu_hi, u + 1)
            v = ps[:, bank, 0:2 * SLOTS].rearrange("p (k s) -> p k s", k=2)
            nc.vector.tensor_tensor(xlo[:, buf, 2 * g:2 * g + 2, :], v, xhi[:, buf, 2 * g:2 * g + 2, :].bitcast(F32),
                                    ALU.subtract).then_inc(psu_lo, 1)

        def scatter_add(m, c, s):
            vec.wait_ge(sc_mm, s + 1)
            for t0, cc, c0, c1 in SEGS:
                if cc == c:
                    w = 1 if t0 >= NL else 0
                    last = nc.vector.scalar_tensor_tensor(out=xr[:, m, t0:t0 + c1 - c0], in0=pt[:, c, c0:c1],
                                                          scalar=mod[:, 5 * KT + m, w:w + 1],
                                                          in1=xr[:, m, t0:t0 + c1 - c0], op0=ALU.mult, op1=ALU.add)
            last.then_inc(sc_add, 1)

        def outer_lo(x, h, n):
            vec.wait_ge(y_hi, n + 1)
            nc.vector.scalar_tensor_tensor(out=ylo[:, :].rearrange(c2, c=2), in0=pu[:, 2 * h:2 * h + 2, :],
                                           scalar=gates[:, x:x + 1],
                                           in1=yhi[:, :].bitcast(F32).rearrange(c2, c=2), op0=ALU.mult,
                                           op1=ALU.subtract).then_inc(y_lo, 1)

        select(0)
        for n in range(AHEAD):
            piece_lo(n, n)
        for g in range(KT // 2):
            gather_lo(g, 0, g % 2, g)

        def experts(i, last_body):
            for st in body_steps():
                kind, x, h, k = st.what
                if kind == "piece":
                    if not (last_body and st.piece + AHEAD >= BODY_PIECES):
                        piece_lo(i * BODY_PIECES + (st.piece + AHEAD), st.piece + AHEAD)
                elif kind == "scatter":
                    scatter_add(8 * h + k // 2, k % 2, i * BODY_SCATTERS + st.scatter)
                elif kind == "slots":
                    u = i * BODY_TURNS + (KT // 2 + st.turn)
                    vec.wait_ge(psu_hi, u + 1)
                    if h == 0:
                        nc.vector.tensor_copy(oht[:, x, 256:512], ps[:, st.turn % 2, 256:512]).then_inc(psu_lo, 1)
                    else:
                        nc.vector.tensor_tensor(gates[:, x:x + 1], ps[:, st.turn % 2, 128:129], own[:, x:x + 1],
                                                ALU.mult).then_inc(psu_lo, 1)
                elif kind == "select":
                    vec.wait_ge(psu_mm, i * BODY_TURNS + (KT // 2 + st.turn))
                    select(i * 2 + (st.pair + 1))
                elif kind == "gather":
                    gather_lo(k, (st.pair + 1) % 2, st.turn % 2, i * BODY_TURNS + (KT // 2 + st.turn))
                elif kind == "turn":
                    vec.wait_ge(psu_hi, i * BODY_TURNS + (KT // 2 + st.turn + 1))
                    nc.vector.tensor_tensor(htlo[:, 4 * h:4 * h + 4, :],
                                            ps[:, st.turn % 2, :].rearrange("p (f s) -> p f s", f=4),
                                            hthi[:, 4 * h:4 * h + 4, :].bitcast(F32), ALU.subtract).then_inc(psu_lo, 1)
                elif kind == "inner":
                    vec.wait_ge(hid_silu, i * BODY_INNERS + (st.inner + 1))
                    nc.vector.tensor_tensor(hid[:, :], hid[:, :], pu[:, 2 * h + 1, :], ALU.mult).then_inc(hid_done, 1)
                elif kind == "outer":
                    outer_lo(x, h, i * BODY_INNERS + st.outer)

        with vec.Fori(0, BODIES - 1) as i:
            experts(i, False)
        experts(BODIES - 1, True)
        for k in range(OLD_ITEMS, 2 * KT):
            if k == KT:
                outer_lo(1, 1, BODIES * BODY_INNERS)
            scatter_add(k // 2, k % 2, BODIES * BODY_SCATTERS + k - OLD_ITEMS)
        for kt in range(KT):
            vec.wait_ge(fin_sq, kt + 1)
            if kt == 0:
                nc.vector.tensor_copy(hfin[:, :], fsq[:, 0, :]).then_inc(fin_sum, 1)
            else:
                vec.wait_ge(fin_sum, kt)
                nc.vector.tensor_tensor(hfin[:, :], hfin[:, :], fsq[:, kt % 2, :], ALU.add).then_inc(fin_sum, 1)
        vec.wait_ge(fin_mm, 1)
        fc = [0]

        def fin(ins):
            fc[0] += 1
            ins.then_inc(fin_c, 1)
            vec.wait_ge(fin_c, fc[0])

        fin(nc.vector.tensor_scalar(f2[:, :].rearrange(c2, c=2), ps[:, :, 0:HALF], EPS, None, ALU.add))
        fin(nc.vector.reciprocal(f3[:, :], f2[:, :]))
        vec.wait_ge(norm_sq, 4)
        fin(nc.vector.tensor_tensor(f3[:, :], f1[:, :], f1[:, :], ALU.mult))
        fin(nc.vector.tensor_tensor(f3[:, :], f3[:, :], f2[:, :], ALU.mult))
        fin(nc.vector.tensor_scalar(f3[:, :], f3[:, :], -0.5, 1.5, ALU.mult, ALU.add))
        fin(nc.vector.tensor_tensor(f1[:, :], f1[:, :], f3[:, :], ALU.mult))
        for kt in range(KT):
            nc.vector.scalar_tensor_tensor(out=xr[:, kt, :], in0=xr[:, kt, :], scalar=norms[:, 2, kt, 0:1],
                                           in1=f1[:, :], op0=ALU.mult, op1=ALU.mult).then_inc(fin_y, 1)

    with nc.Block() as block:
        @block.sync
        def _(sp):
            sync_program(sp)

        @block.gpsimd
        def _(pool):
            pool_program(pool)

        @block.tensor
        def _(pe):
            tensor_program(pe)

        @block.scalar
        def _(act):
            scalar_program(act)

        @block.vector
        def _(vec):
            vector_program(vec)


def laid_out(x):
    import numpy as np

    def f(v):
        return np.ascontiguousarray(v)

    def blocks(w, m=1):
        k, n = w.shape
        v = w.reshape(k // 128, 128, n // 128 // m, m, 128).transpose(2, 1, 3, 0, 4)
        return f(v).reshape(n // 128 // m, 128, -1)

    def per_channel(v):
        return f(np.asarray(v).reshape(-1, 128).T)

    w = {k: np.asarray(v) for k, v in x.items()}
    tok = np.concatenate([w["x_sample"][0], w["x_prompt"][0]], axis=0)
    o = {}
    o["x"] = f(tok.reshape(N, KT, 128).transpose(2, 1, 0))
    o["cond"] = f(np.stack([per_channel(w["c"][0]), per_channel(w["c_ctx"])], axis=2))
    o["w_ada"] = blocks(w["w_ada"][0])
    o["b_ada"] = per_channel(w["b_ada"][0])
    o["norms"] = f(np.stack([np.repeat(per_channel(g)[:, :, None], 2, axis=2)
                             for g in (w["norm1_g"][0], w["norm2_g"][0], w["final_norm_g"])], axis=1))
    win = blocks(w["w_in"][0])
    glu = 2 * CT
    q0, k0, v0, ga0 = glu, glu + NH, glu + NH + NKV, glu + NH + 2 * NKV
    order = [*range(v0, v0 + NKV), *range(k0, k0 + NKV), *range(q0, q0 + NH)]
    for m in range(CT):
        order += [CT + m, m]
    order += list(range(ga0, ga0 + 2 * KT))
    o["w_in"] = f(win[order])
    o["taps"] = f(w["conv_dw"][0].T.reshape(CT, 128, TAPS).transpose(1, 0, 2))
    o["convp"] = f(np.stack([per_channel(w[n][0]) for n in ("conv_dw_b", "conv_ln_g", "conv_ln_b")], axis=1))
    o["sinks"] = f(np.broadcast_to(w["attn_sink"][0][None], (128, NH)))
    o["cache_k"] = f(w["cache_k"][0, 0].transpose(1, 2, 0))
    o["cache_v"] = f(w["cache_v"][0, 0].reshape(2, 128, NKV, HD).transpose(2, 1, 0, 3))
    o["w_conv_out"] = blocks(w["w_conv_out"][0], 2)
    o["w_attn_out"] = blocks(w["w_attn_out"][0])
    o["w_out"] = blocks(w["w_out"][0])
    o["w_router"] = f(w["w_router"][0].reshape(KT, 128, NE).transpose(1, 0, 2))
    o["b_router"] = f(w["b_router"][0].reshape(NE, 1))
    def columns(w, m):
        k, n = w.shape
        return w.reshape(k // 128, 128, n // m, m).transpose(2, 0, 1, 3)

    ew = []
    for e in range(NE):
        g, u = columns(w["w_exp_gate"][0, e], 512), columns(w["w_exp_up"][0, e], 512)
        both = np.concatenate([g, u], axis=3).reshape(2 * KT, 128, 1024)
        down = columns(w["w_exp_down"][0, e], 1024).reshape(2 * FT, 128, 1024)
        v = np.concatenate([both, down])
        ew.append(v.reshape(PIECES // 2, 2, 128, 1024).transpose(0, 2, 1, 3).reshape(PIECES // 2, 128, UNIT))
    o["w_experts"] = f(np.concatenate(ew))
    own = np.zeros((128, 2), np.float32)
    own[:CAP, 0] = 1
    own[128 - CAP:, 1] = 1
    o["own"] = own
    quarter = HD // 4
    inv = 10000.0 ** (-np.arange(quarter, dtype=np.float32) / np.float32(quarter))
    t = np.arange(NL)
    ang = [(p[None, :].astype(np.float32) * inv[:, None].astype(np.float32)).astype(np.float32)
           for p in (t // 64, t % 64)]
    cos, sin = np.ones((128, N), np.float32), np.zeros((128, N), np.float32)
    for b, an in enumerate(ang):
        for s in range(2):
            rows = slice(64 * b + 32 * s, 64 * b + 32 * s + 32)
            cos[rows, :NL] = np.cos(an)
            sin[rows, :NL] = np.sin(an) if s == 0 else -np.sin(an)
    o["cos"], o["sin"] = cos, sin
    q, k = np.arange(128)[:, None], np.arange(384)[None, :] - 128
    o["mask"] = np.where(np.abs(q - k) <= 128, 0.0, NEG).astype(np.float32)
    tri = (np.arange(128)[:, None] <= np.arange(128)[None, :]).astype(np.float32)
    o["triangle"] = f(np.stack([tri, np.ones((128, 128), np.float32)], axis=1))
    o["iota"] = np.broadcast_to(np.arange(1, 65, dtype=np.float32)[None], (128, 64)).copy()
    return o


def kernel(**inputs):
    import numpy as np
    import concourse.bacc as bacc
    from concourse.bass_utils import run_bass_kernel_spmd

    nc = bacc.Bacc("TRN2", target_bir_lowering=False, num_devices=1)
    host = laid_out(inputs)
    arrays, args = {}, {}
    for name, v in host.items():
        arrays[f"in_{name}"] = v
        args[name] = nc.dram_tensor(f"in_{name}", v.shape, F32, kind="ExternalInput").ap()
    outs = {"y": (KT, 128, N), "k": (NKV, 128, NC), "v": (NKV, 128, NC)}
    oaps = {n: nc.dram_tensor(f"out_{n}", s, F32, kind="ExternalOutput").ap() for n, s in outs.items()}
    build(nc, args, oaps)
    r = run_bass_kernel_spmd(nc, [arrays], core_ids=[0]).results[0]
    y = np.asarray(r["out_y"]).transpose(2, 0, 1).reshape(N, D)
    k = np.asarray(r["out_k"]).transpose(2, 0, 1)[None, None]
    v = np.asarray(r["out_v"]).transpose(2, 0, 1)[None, None]
    return (np.ascontiguousarray(y[NL:])[None], np.ascontiguousarray(y[:NL])[None],
            np.ascontiguousarray(k), np.ascontiguousarray(v))
```
